# Optimizing a Trainium2 kernel written in Bass

```python
import math
import jax, jax.numpy as jnp
from jax import lax
import numpy as np

D_MODEL = 1024
BATCH = 1
SEQ = 512
DEPTH = 1

D_MIX = D_MODEL
SSD_HEADS = 8
SSD_HEAD_DIM = 64
D_SSD = SSD_HEADS * SSD_HEAD_DIM
SSD_GROUPS = 2
SSD_HEADS_PER_GROUP = SSD_HEADS // SSD_GROUPS
D_STATE = 128
CONV_WIDTH = 4
SSD_CHUNK = 128
D_CONV = D_SSD + 2 * SSD_GROUPS * D_STATE
ATTN_Q_HEADS = 8
ATTN_KV_HEADS = 2
ATTN_Q_PER_KV = ATTN_Q_HEADS // ATTN_KV_HEADS
ATTN_HEAD_DIM = 64
D_ATTN = ATTN_Q_HEADS * ATTN_HEAD_DIM
D_KV = ATTN_KV_HEADS * ATTN_HEAD_DIM
WINDOW = 128
ATTN_BLOCK = 128
REL_BUCKETS = 32
REL_MAX_DIST = 128
D_PROJ = D_SSD + D_CONV + SSD_HEADS + D_ATTN + 2 * D_KV
N_EXPERTS = 32
TOP_K = 4
D_EXPERT = D_MODEL
SWIGLU_LIMIT = 7.0
SWIGLU_ALPHA = 1.702
MOE_BLOCK = 128
RMS_EPS = 1e-5

kernel_name = "hymba_ssd_swa_sink_moe_block"

def rmsnorm(x, g):
    xf = x.astype(jnp.float32)
    y = xf * lax.rsqrt(jnp.mean(xf * xf, axis=-1, keepdims=True) + RMS_EPS)
    return (y * g.astype(jnp.float32)).astype(x.dtype)

def causal_depthwise_conv(u, w, b):
    k_width, chans = w.shape
    out = lax.conv_general_dilated(
        u, w[:, None, :].astype(u.dtype), window_strides=(1,),
        padding=[(k_width - 1, 0)], dimension_numbers=("NWC", "WIO", "NWC"),
        feature_group_count=chans)
    return out + b.astype(u.dtype)

def ssd_group(z, xbc, dt_raw, conv_w, conv_b, dt_bias, a_log, d_skip, norm_g):
    bsz, seq = z.shape[0], z.shape[1]
    nc = seq // SSD_CHUNK
    G, R, P, N, L = SSD_GROUPS, SSD_HEADS_PER_GROUP, SSD_HEAD_DIM, D_STATE, SSD_CHUNK
    xbc = jax.nn.silu(causal_depthwise_conv(xbc, conv_w, conv_b))
    xs = xbc[..., :D_SSD]
    bm = xbc[..., D_SSD:D_SSD + G * N].reshape(bsz, nc, L, G, N)
    cm = xbc[..., D_SSD + G * N:].reshape(bsz, nc, L, G, N)
    x = xs.reshape(bsz, nc, L, G, R, P)
    dt = jax.nn.softplus(dt_raw.astype(jnp.float32) + dt_bias.astype(jnp.float32))
    a = -jnp.exp(a_log.astype(jnp.float32))
    dt_c = dt.reshape(bsz, nc, L, G, R)
    xdt = x * dt_c[..., None]
    a_dt = jnp.transpose(dt_c * a.reshape(G, R), (0, 3, 4, 1, 2))
    a_cum = jnp.cumsum(a_dt, axis=-1)
    seg = a_cum[..., :, None] - a_cum[..., None, :]
    causal = jnp.tril(jnp.ones((L, L), dtype=bool))
    decay = jnp.exp(jnp.where(causal, seg, -jnp.inf))
    cb = jnp.einsum("bclgn,bcsgn->bgcls", cm, bm)
    y_diag = jnp.einsum("bgrcls,bcsgrp->bclgrp", cb[:, :, None] * decay, xdt)
    decay_to_end = jnp.exp(a_cum[..., -1:] - a_cum)
    states = jnp.einsum("bclgn,bgrcl,bclgrp->bcgrpn", bm, decay_to_end, xdt)
    chunk_decay = jnp.exp(a_cum[..., -1])

    def step(h, inp):
        st, dec = inp
        return h * dec[..., None, None] + st, h

    h0 = jnp.zeros(states.shape[:1] + states.shape[2:], states.dtype)
    _, prev = lax.scan(step, h0, (jnp.moveaxis(states, 1, 0), jnp.moveaxis(chunk_decay, 3, 0)))
    prev = jnp.moveaxis(prev, 0, 1)
    y_off = jnp.einsum("bclgn,bcgrpn,bgrcl->bclgrp", cm, prev, jnp.exp(a_cum))
    y = y_diag + y_off + x * d_skip.reshape(G, R)[:, :, None]
    y = y.reshape(bsz, seq, D_SSD).astype(z.dtype)
    return rmsnorm(y * jax.nn.silu(z), norm_g)

def t5_bucket(dist):
    max_exact = REL_BUCKETS // 2
    is_small = dist < max_exact
    d = jnp.maximum(dist, 1).astype(jnp.float32)
    large = max_exact + (jnp.log(d / max_exact) / math.log(REL_MAX_DIST / max_exact)
                         * (REL_BUCKETS - max_exact)).astype(jnp.int32)
    large = jnp.minimum(large, REL_BUCKETS - 1)
    return jnp.where(is_small, dist, large)

def swa_group(q, k, v, sinks, rel_bias):
    bsz, seq = q.shape[0], q.shape[1]
    L = ATTN_BLOCK
    nb = seq // L
    HK, G, Dh = ATTN_KV_HEADS, ATTN_Q_PER_KV, ATTN_HEAD_DIM
    qb = q.reshape(bsz, nb, L, HK, G, Dh)
    kb = k.reshape(bsz, nb, L, HK, Dh)
    vb = v.reshape(bsz, nb, L, HK, Dh)
    kk = jnp.concatenate([jnp.concatenate([jnp.zeros_like(kb[:, :1]), kb[:, :-1]], axis=1), kb], axis=2)
    vv = jnp.concatenate([jnp.concatenate([jnp.zeros_like(vb[:, :1]), vb[:, :-1]], axis=1), vb], axis=2)
    s = jnp.einsum("bnqhgd,bnkhd->bnhgqk", qb, kk).astype(jnp.float32) * (1.0 / math.sqrt(Dh))
    dist = L + jnp.arange(L)[:, None] - jnp.arange(2 * L)[None, :]
    in_window = (dist >= 0) & (dist < WINDOW)
    bias = rel_bias.astype(jnp.float32)[t5_bucket(jnp.clip(dist, 0, REL_MAX_DIST))]
    bias = jnp.transpose(bias.reshape(L, 2 * L, HK, G), (2, 3, 0, 1))
    prev_ok = (jnp.arange(nb)[:, None] > 0) | (jnp.arange(2 * L)[None, :] >= L)
    mask = in_window[None] & prev_ok[:, None, :]
    s = jnp.where(mask[None, :, None, None], s + bias[None, None], -jnp.inf)
    sink = sinks.astype(jnp.float32).reshape(HK, G)[None, None, :, :, None, None]
    m = jnp.maximum(jnp.max(s, axis=-1, keepdims=True), sink)
    p = jnp.exp(s - m)
    p = p / (jnp.sum(p, axis=-1, keepdims=True) + jnp.exp(sink - m))
    o = jnp.einsum("bnhgqk,bnkhd->bnqhgd", p.astype(vv.dtype), vv)
    return o.reshape(bsz, seq, D_ATTN)

def clamped_swiglu(hid):
    x_glu = jnp.minimum(hid[..., :D_EXPERT], SWIGLU_LIMIT)
    x_lin = jnp.clip(hid[..., D_EXPERT:], -SWIGLU_LIMIT, SWIGLU_LIMIT)
    return x_glu * jax.nn.sigmoid(SWIGLU_ALPHA * x_glu) * (x_lin + 1.0)

def moe_ffn(u, w_router, b_router, w1, b1, w2, b2):
    bsz, seq, d = u.shape
    T = bsz * seq
    xt = u.reshape(T, d)
    logits = (xt @ w_router + b_router).astype(jnp.float32)
    top_val, top_idx = lax.top_k(logits, TOP_K)
    gate = jax.nn.softmax(top_val, axis=-1)
    e_flat = top_idx.reshape(-1).astype(jnp.int32)
    tok_flat = jnp.repeat(jnp.arange(T, dtype=jnp.int32), TOP_K)
    g_flat = gate.reshape(-1)
    order = jnp.argsort(e_flat)
    e_sorted = e_flat[order]
    counts = jnp.bincount(e_flat, length=N_EXPERTS)
    starts = jnp.cumsum(counts) - counts
    padded = ((counts + MOE_BLOCK - 1) // MOE_BLOCK) * MOE_BLOCK
    padded_ends = jnp.cumsum(padded)
    padded_starts = padded_ends - padded
    n_assign = T * TOP_K
    dest = padded_starts[e_sorted] + jnp.arange(n_assign) - starts[e_sorted]
    P = n_assign + N_EXPERTS * MOE_BLOCK
    row_tok = jnp.full((P,), T, dtype=jnp.int32).at[dest].set(tok_flat[order])
    row_gate = jnp.zeros((P,), jnp.float32).at[dest].set(g_flat[order])
    nblk = P // MOE_BLOCK
    blk_expert = jnp.minimum(
        jnp.searchsorted(padded_ends, jnp.arange(nblk) * MOE_BLOCK, side="right"), N_EXPERTS - 1)
    x_pad = jnp.concatenate([xt, jnp.zeros((1, d), xt.dtype)], axis=0)
    xs = x_pad[row_tok].reshape(nblk, MOE_BLOCK, d)

    def expert_block(args):
        xb, e = args
        hid = clamped_swiglu(xb @ w1[e] + b1[e])
        return hid @ w2[e] + b2[e]

    ys = lax.map(expert_block, (xs, blk_expert)).reshape(P, d)
    ys = ys * row_gate[:, None].astype(ys.dtype)
    out = jax.ops.segment_sum(ys, row_tok, num_segments=T + 1)[:T]
    return out.reshape(bsz, seq, d)

def setup_inputs(seed: int = 0) -> dict:
    key = jax.random.key(seed)
    ks = jax.random.split(key, 24)
    f32 = jnp.float32
    nrm = lambda k, shape, scale: jax.random.normal(k, shape, f32) * scale
    gain = lambda k, shape: 1.0 + 0.05 * jax.random.normal(k, shape, f32)
    dt0 = jnp.exp(jax.random.uniform(ks[5], (DEPTH, SSD_HEADS), f32, math.log(1e-3), math.log(1e-1)))
    return {
        "x": nrm(ks[0], (BATCH, SEQ, D_MODEL), 1.0),
        "norm_mix_g": gain(ks[1], (DEPTH, D_MODEL)),
        "w_in": nrm(ks[2], (DEPTH, D_MODEL, D_PROJ), D_MODEL ** -0.5),
        "conv_w": nrm(ks[3], (DEPTH, CONV_WIDTH, D_CONV), CONV_WIDTH ** -0.5),
        "conv_b": nrm(ks[4], (DEPTH, D_CONV), 0.02),
        "dt_bias": jnp.log(jnp.expm1(dt0)),
        "a_log": jnp.log(jax.random.uniform(ks[6], (DEPTH, SSD_HEADS), f32, 1.0, 16.0)),
        "d_skip": gain(ks[7], (DEPTH, SSD_HEADS)),
        "ssd_norm_g": gain(ks[8], (DEPTH, D_SSD)),
        "attn_sinks": nrm(ks[9], (DEPTH, ATTN_Q_HEADS), 0.5),
        "rel_bias": nrm(ks[10], (REL_BUCKETS, ATTN_Q_HEADS), 0.5),
        "attn_norm_g": gain(ks[11], (DEPTH, D_ATTN)),
        "w_out": nrm(ks[12], (DEPTH, D_MIX, D_MODEL), D_MIX ** -0.5),
        "norm_ffn_g": gain(ks[13], (DEPTH, D_MODEL)),
        "w_router": nrm(ks[14], (DEPTH, D_MODEL, N_EXPERTS), D_MODEL ** -0.5),
        "b_router": nrm(ks[15], (DEPTH, N_EXPERTS), 0.01),
        "w1": nrm(ks[16], (DEPTH, N_EXPERTS, D_MODEL, 2 * D_EXPERT), D_MODEL ** -0.5),
        "b1": nrm(ks[17], (DEPTH, N_EXPERTS, 2 * D_EXPERT), 0.02),
        "w2": nrm(ks[18], (DEPTH, N_EXPERTS, D_EXPERT, D_MODEL), D_EXPERT ** -0.5),
        "b2": nrm(ks[19], (DEPTH, N_EXPERTS, D_MODEL), 0.02),
        "norm_final_g": gain(ks[20], (D_MODEL,)),
    }

def reference(x, norm_mix_g, w_in, conv_w, conv_b, dt_bias, a_log, d_skip, ssd_norm_g,
              attn_sinks, rel_bias, attn_norm_g, w_out, norm_ffn_g, w_router, b_router,
              w1, b1, w2, b2, norm_final_g):
    h = x
    o1 = D_SSD
    o2 = o1 + D_CONV
    o3 = o2 + SSD_HEADS
    o4 = o3 + D_ATTN
    o5 = o4 + D_KV
    for layer in range(DEPTH):
        u = rmsnorm(h, norm_mix_g[layer])
        proj = u @ w_in[layer]
        z, xbc, dt_raw = proj[..., :o1], proj[..., o1:o2], proj[..., o2:o3]
        q, k, v = proj[..., o3:o4], proj[..., o4:o5], proj[..., o5:]
        y_ssd = ssd_group(z, xbc, dt_raw, conv_w[layer], conv_b[layer], dt_bias[layer],
                          a_log[layer], d_skip[layer], ssd_norm_g[layer])
        y_attn = rmsnorm(swa_group(q, k, v, attn_sinks[layer], rel_bias), attn_norm_g[layer])
        h = h + jnp.concatenate([y_ssd, y_attn], axis=-1) @ w_out[layer]
        h = h + moe_ffn(rmsnorm(h, norm_ffn_g[layer]), w_router[layer], b_router[layer],
                        w1[layer], b1[layer], w2[layer], b2[layer])
    return rmsnorm(h, norm_final_g)


_drawn_inputs = setup_inputs


def setup_inputs(seed=0):
    import zlib

    import numpy as np

    out = dict(_drawn_inputs(seed))
    spreads = {}
    factors = {'attn_sinks': 4.09, 'b1': 6.849, 'b2': 7.985}
    for name, (base, spread) in spreads.items():
        noise = np.random.default_rng([zlib.crc32(name.encode()), seed]).standard_normal(out[name].shape)
        drawn = base * np.exp(spread * noise) if base else spread * noise
        out[name] = __import__('jax').numpy.asarray(drawn.astype(out[name].dtype))
    for name, factor in factors.items():
        out[name] = (out[name] * factor).astype(out[name].dtype)
    return out
```

```python
import math
from contextlib import ExitStack

import numpy as np

import concourse.bass as bass
from concourse import mybir

F32 = mybir.dt.float32
F32R = mybir.dt.float32r
U32 = mybir.dt.uint32
ALU = mybir.AluOpType
ACT = mybir.ActivationFunctionType
AX = mybir.AxisListType

P = 128
T = 512
TT = T // P
D = 1024
DK = D // P
D_SSD = 512
HEADS = 8
HD = 64
STATE = 128
E = 32
TOPK = 4
EPS = 1e-5
NEG = -1e30
BUCKETS = 32
WINDOW = 128
CHUNK = 2048
FW = 3 * P - 1

N_X = 2
N_XBC, N_Z, N_KV, N_Q = 4, 2, 1, 2
N_IN = N_XBC + N_Z + N_KV + N_Q
N_OUT = 4
N_PRO = N_X + N_IN + N_OUT
C_IN = N_X
C_OUT = N_X + N_IN
PRO_SLOTS = 9
PER_EXPERT = 12
SLOTS = 12
EXPERT_SLOT = [(6 + m) % PRO_SLOTS for m in range(PRO_SLOTS)] + [9, 10, 11]
SPLITS = 3


def t5_bucket(dist):
    max_exact = BUCKETS // 2
    d = np.maximum(dist, 1).astype(np.float32)
    large = max_exact + (np.log(d / np.float32(max_exact)) / np.float32(math.log(128 / max_exact))
                         * np.float32(BUCKETS - max_exact)).astype(np.int32)
    return np.where(dist < max_exact, dist, np.minimum(large, BUCKETS - 1))


def shape_constants():
    i = np.arange(P)
    f = np.float32
    band = np.zeros((BUCKETS + 1, FW), f)
    for j in range(FW):
        dist = 2 * P - 1 - j
        if 0 <= dist < WINDOW:
            band[t5_bucket(np.array(dist)), j] = 1
        else:
            band[BUCKETS, j] = 1
    tokens = (i[:, None] + P * np.arange(TT)[None, :]).astype(f)
    parts = {
        "ident": np.eye(P, dtype=f),
        "incl": (i[:, None] <= i[None, :]).astype(f),
        "strict": (i[:, None] < i[None, :]).astype(f),
        "ones": np.ones((P, P), f),
        "slots": np.broadcast_to(i.astype(f), (P, P)),
        "negmask": np.where(i[:, None] > i[None, :], f(NEG), f(0)),
        "band": np.concatenate([band, np.zeros((P - BUCKETS - 1, FW), f)]),
        "neg": np.full((P, HEADS), NEG, f),
        "experts": np.broadcast_to(np.arange(E, dtype=f), (P, E)),
        "tokens": tokens,
        "trash": (T + i[:, None]).astype(f),
        "rows2e": (i[:, None] % E == np.arange(E)[None, :]).astype(f) * (i[:, None] < 2 * E),
    }
    at, where = 0, {}
    for name, a in parts.items():
        where[name] = (at, a.shape[1])
        at += a.shape[1]
    return np.ascontiguousarray(np.concatenate(list(parts.values()), 1).astype(f)), where


MAIN_CONSTS = ("ident", "strict", "ones", "slots", "experts", "tokens", "trash", "rows2e")
MIXER_CONSTS = ("incl", "negmask")
VECTORS = (("norm_mix_g", DK), ("conv_w", 32), ("conv_b", 8), ("mix_g", DK), ("dt_bias", HEADS),
           ("a_log", HEADS), ("d_skip", HEADS), ("sinks", HEADS), ("b_router", E))


def build(nc, stream, x, w_dt, vectors, consts, rel_bias, norm_ffn_g, norm_final_g, w_router,
          b1, b2, out):
    _, where = shape_constants()

    band_dram = nc.dram_tensor("band_dram", [P, HEADS * FW], F32)
    u_dram = nc.dram_tensor("u_dram", [T, D], F32)
    acc_dram = nc.dram_tensor("acc_dram", [T + P, D], F32)

    base = (nc.sbuf_base + 63) // 64 * 64
    sizes = {}

    def at(name, shape, dtype, offset):
        sizes[name] = (offset, offset + 4 * int(np.prod(shape[1:])))
        return nc.alloc_sbuf_tensor_at(name, shape, dtype, offset=base + offset)

    RING, HI, LO = 0, 73728, 98304
    SMALL = 122880
    A = SMALL + 5632
    F = A + 24576
    ring = [at(f"ring{s}", [P, CHUNK], F32, RING + 8192 * s) for s in range(PRO_SLOTS)] + \
           [at(f"ring{s}", [P, CHUNK], F32, A + 8192 * (s - PRO_SLOTS)) for s in range(PRO_SLOTS, SLOTS)]
    w_hi = [at(f"w_hi{s}", [P, CHUNK], F32R, HI + 8192 * s) for s in range(SPLITS)]
    w_lo = [at(f"w_lo{s}", [P, CHUNK], F32R, LO + 8192 * s) for s in range(SPLITS)]

    off = SMALL
    main_w = sum(where[n][1] for n in MAIN_CONSTS)
    vec_w = sum(w for _, w in VECTORS)
    main = at("main", [P, main_w], F32, off); off += (4 * main_w + 31) // 32 * 32
    vec = at("vec", [P, vec_w], F32, off); off += (4 * vec_w + 31) // 32 * 32
    slot_rhs = at("slot_rhs", [P, TT, E, 4], F32, off); off += 16 * TT * E
    pos = at("pos", [P, TT, E], F32, off); off += 4 * TT * E
    smalls_end = off
    assert off <= A, (off, A)
    const = {}
    col = 0
    for n in MAIN_CONSTS:
        const[n] = main[:, col:col + where[n][1]]
        col += where[n][1]
    v = {}
    col = 0
    for n, w in VECTORS:
        v[n] = vec[:, col:col + w]
        col += w
    ident = const["ident"]

    xg_hi = at("xg_hi", [P, DK, T], F32R, A)
    xg_lo = at("xg_lo", [P, DK, T], F32R, A + 16384)
    B = A + 32768
    xbc = at("xbc", [P, 8, T], F32, B)
    zs = at("zs", [P, TT, D_SSD], F32, B + 16384)
    q_t = at("q_t", [P, 4, T], F32, B + 24576)
    sq = at("sq", [P, DK, T], F32, B + 16384)
    k_t = at("k_t", [P, P + T], F32, B + 32768)
    v_tok = at("v_tok", [P, TT + 1, P], F32, B + 35328)
    conv_in = at("conv_in", [P, 2, T + 4], F32, B + 37888)
    conv_acc = at("conv_acc", [P, 2, T], F32, B + 42016)
    rstd_row = at("rstd_row", [P, T], F32, B + 46112)
    off = B + 48160
    band = at("band", [BUCKETS + 1, FW + 1], F32, off); off += 4 * (FW + 1)
    wdt = at("wdt", [P, DK, HEADS], F32, off); off += 256
    wdt_hi = at("wdt_hi", [P, DK, HEADS], F32R, off); off += 256
    wdt_lo = at("wdt_lo", [P, DK, HEADS], F32R, off); off += 256
    rstd_tok = at("rstd_tok", [P, TT], F32, off); off += 32
    assert off - A <= 83456, off - A
    band_rows = at("band_rows", [HEADS, FW + 1], F32, B)
    dt_row = at("dt_row", [HEADS, T], F32, B + 24576)
    rel = at("rel", [BUCKETS + 1, HEADS], F32, B + 46112)

    S = HI
    x_tok = at("x_tok", [P, D_SSD], F32, S)
    x_tok2 = at("x_tok2", [P, D_SSD], F32, S + 2048)
    b_tok = at("b_tok", [P, 2, STATE], F32, S + 4096)
    b_tok2 = at("b_tok2", [P, 2, STATE], F32, S + 5120)
    x_toks, b_toks = [x_tok, x_tok2], [b_tok, b_tok2]
    xdt = at("xdt", [P, D_SSD], F32, S + 6144)
    xdd = at("xdd", [P, D_SSD], F32, S + 8192)
    xskip = at("xskip", [P, D_SSD], F32, S + 10240)
    decay = [at(f"decay{g}", [P, 4, P], F32, S + 12288 + 2048 * g) for g in range(2)]
    m_t = [at(f"m_t{g}", [P, 4, P], F32, S + 16384 + 2048 * g) for g in range(2)]
    state = at("state", [P, D_SSD], F32, S + 20480)
    y_tmp = at("y_tmp", [P, D_SSD], F32, S + 22528)
    scores = [at(f"scores{i}", [P, 2, 2 * P], F32, S + 24576 + 2048 * i) for i in range(2)]
    probs = [at(f"probs{i}", [P, 2, 2 * P], F32, S + 28672 + 2048 * i) for i in range(2)]
    probs_t = [at(f"probs_t{i}", [P, 4, P], F32, S + 32768 + 2048 * i) for i in range(2)]
    incl = at("incl", [P, P], F32, S + 36864)
    negmask = at("negmask", [P, P], F32, S + 37376)
    off = S + 37888

    def small(name, cols, dtype=F32):
        nonlocal off
        t = at(name, [P, cols], dtype, off)
        off += (4 * cols + 31) // 32 * 32
        return t

    dt_raw, dt_e, dt_u, dt_d, dt_l, dt, adt, acum, nacum, eacum, dend, dtot = (
        small(n, 32) for n in ("dt_raw", "dt_e", "dt_u", "dt_d", "dt_l", "dt", "adt", "acum",
                               "nacum", "eacum", "dend", "dtot"))
    a_neg = small("a_neg", HEADS)
    smax = small("smax", 32)
    nmax = small("nmax", 32)
    sinkd = small("sinkd", 32)
    psums = small("psums", 32)
    esink = small("esink", 32)
    rden = small("rden", 32)
    ssq = small("ssq", 8)
    rms = small("rms", 8)
    sq_junk = small("sq_junk", D_SSD)
    assert off <= SMALL, off
    bias = at("bias", [P, HEADS, 2 * P], F32, B + 37888)
    mix = at("mix", [P, TT, D], F32, A + 16384)
    mix_hi = at("mix_hi", [P, DK, T], F32R, B)
    mix_lo = at("mix_lo", [P, DK, T], F32R, B + 16384)
    h = at("h", [P, TT, D], F32, A)
    u2 = [at(f"u2_{i}", [P, D], F32, A + 16384 + 4096 * i) for i in range(2)]
    u2_t = [at(f"u2_t{i}", [P, DK, P], F32, A + 24576 + 4096 * i) for i in range(2)]
    R = B + 32768
    ffn_g = at("ffn_g", [P, D], F32, R)
    wr = at("wr", [P, DK, E], F32, R + 4096)
    off = R + 5120
    logits = small("logits", TT * E)
    top = small("top", TT * 8)
    top_idx = small("top_idx", TT * 8, U32)
    top_f = small("top_f", TT * 8)
    gexp = small("gexp", TT * 4)
    gsum = small("gsum", TT)
    gate = small("gate", TT * 4)
    pick = small("pick", TT * E)
    gpick = small("gpick", TT * E)
    mask = small("mask", TT * E)
    gates = small("gates", TT * E)
    ssq2 = small("ssq2", TT)
    rms2 = small("rms2", TT)
    gates_t = at("gates_t", [E, TT, P], F32, off); off += 2048
    b2_sb = at("b2_sb", [E, D], F32, off); off += 4096
    assert off <= R + 14464, off - R
    y_sb = [at(f"y_sb{i}", [P, D], F32, F + 4096 * i) for i in range(2)]
    b1_hl = at("b1_hl", [2 * E, 2 * D], F32R, B)
    xe = [at(f"xe{i}", [P, D], F32, B + 8192 + 4096 * i) for i in range(2)]
    xe_hi = [at(f"xe_hi{i}", [P, DK, P], F32R, B + 16384 + 4096 * i) for i in range(2)]
    xe_lo = [at(f"xe_lo{i}", [P, DK, P], F32R, B + 24576 + 4096 * i) for i in range(2)]
    b1_raw = at("b1_raw", [2 * E, 2 * D], F32, B + 24576)
    glu = at("glu", [P, T], F32, R)
    lin = at("lin", [P, T], F32, R + 2048)
    sig = at("sig", [P, T], F32, R + 4096)
    hid_hi = [at(f"hid_hi{i}", [P, 4, P], F32R, R + 6144 + 2048 * i) for i in range(2)]
    hid_lo = [at(f"hid_lo{i}", [P, 4, P], F32R, R + 10240 + 2048 * i) for i in range(2)]
    onehot = at("onehot", [P, TT, P], F32, R + 14464)
    sel = [at(f"sel{i}", [2 * E, P], F32R, R + 16512 + 512 * i) for i in range(2)]
    off = R + 17536
    slot_gate = small("slot_gate", E)
    slot_token = small("slot_token", E, U32)
    slot_row = small("slot_row", E, U32)
    assert off <= A + 83456, off - A

    off = smalls_end
    power = small("power", 4)
    n_max = small("n_max", 1)
    n_max_u = small("n_max_u", 1, U32)
    valid = small("valid", 1)
    assert off <= A, off
    off = A + 83456
    fin_ssq_t = small("fin_ssq_t", TT)
    fin_rms_t = small("fin_rms_t", TT)
    assert base + off <= nc.sbuf_usable_end
    fin = [at(f"fin{t}", [P, D], F32, RING + 4096 * t) for t in range(TT)]
    fin_g = at("fin_g", [P, D], F32, RING + 16384)
    fin_junk = at("fin_junk", [P, D], F32, RING + 20480)

    psum = nc.alloc_psum_tensor("psum", [P, 8, 512], F32)
    bank = [psum[:, i, :] for i in range(8)]

    with ExitStack() as ctx:
        sems = {}

        def sem(name):
            sems[name] = ctx.enter_context(nc.semaphore(name))
            return sems[name]

        const_loaded = sem("const_loaded")
        w_loaded = [sem(f"w_loaded{s}") for s in range(SLOTS)]
        band_stored, bias_loaded, scan_consts_loaded, h_loaded = map(
            sem, ("band_stored", "bias_loaded", "scan_consts_loaded", "h_loaded"))
        router_loaded, b1_loaded, acc_stored = map(sem, ("router_loaded", "b1_loaded", "acc_stored"))
        u_stored = [sem(f"u_stored_{i}") for i in range(2)]
        xg_hi_done, xg_lo_done, sq_done, hi_done, lo_done, chunk_used = map(
            sem, ("xg_hi_done", "xg_lo_done", "sq_done", "hi_done", "lo_done", "chunk_used"))
        vec_loaded, band_ps, band_made, pads_made, ss_ps, rstd_made, rstd_t_ps, rstd_tok_made = map(
            sem, ("vec_loaded", "band_ps", "band_made", "pads_made", "ss_ps", "rstd_made",
                  "rstd_t_ps", "rstd_tok_made"))
        dt_row_made, dt_t_ps = map(sem, ("dt_row_made", "dt_t_ps"))
        proj_evac, z_made, v_made, conv_done, silu_done, wdt_hi_done, wdt_lo_done, dt_ps = map(
            sem, ("proj_evac", "z_made", "v_made", "conv_done", "silu_done", "wdt_hi_done",
                  "wdt_lo_done", "dt_ps"))
        dve_step, act_step, pool_step = map(sem, ("dve_step", "act_step", "pool_step"))
        dt_arg, dt_exp, dt_one, dt_log, a_exp, adt_made, cum_ps, cum_made, cum_exp = map(
            sem, ("dt_arg", "dt_exp", "dt_one", "dt_log", "a_exp", "adt_made", "cum_ps",
                  "cum_made", "cum_exp"))
        tok_ps, tok_made, xs_made, bc_ps, decay_made, m_made, y_ps, y_read, state_made = map(
            sem, ("tok_ps", "tok_made", "xs_made", "bc_ps", "decay_made", "m_made", "y_ps",
                  "y_read", "state_made"))
        sc_ps, sc_read, nmax_made, exp_made, pt_ps, pt_made, o_ps, o_read = map(
            sem, ("sc_ps", "sc_read", "nmax_made", "exp_made", "pt_ps", "pt_made", "o_ps", "o_read"))
        ssq_made, mean_made, rms_made, normed = map(
            sem, ("ssq_made", "mean_made", "rms_made", "normed"))
        ms_made, rms_root = map(sem, ("ms_made", "rms_root"))
        mix_ps, mix_hi_done, mix_lo_done, h_made = map(
            sem, ("mix_ps", "mix_hi_done", "mix_lo_done", "h_made"))
        h_ssq, u_made, u_t_ps, u_t_made, logit_ps = map(
            sem, ("h_ssq", "u_made", "u_t_ps", "u_t_made", "logit_ps"))
        top_made, top_exp, mask_made, pos_ps, pos_made, gates_t_ps, gates_t_made = map(
            sem, ("top_made", "top_exp", "mask_made", "pos_ps", "pos_made", "gates_t_ps",
                  "gates_t_made"))
        rhs_filled, count_made, b2_ps, acc_made, b1_hi_done, b1_lo_done, h_rms = map(
            sem, ("rhs_filled", "count_made", "b2_ps", "acc_made", "b1_hi_done", "b1_lo_done", "h_rms"))
        out_stored = sem("out_stored")
        onehot_made, sel_made, slot_ps, slot_info = map(
            sem, ("onehot_made", "sel_made", "slot_ps", "slot_info"))
        xe_loaded = [sem(f"xe_loaded{i}") for i in range(2)]
        xt_ps, xt_hi_made, xt_lo_made, glu_made, lin_made, u_half, sig_made, hid_made = map(
            sem, ("xt_ps", "xt_hi_made", "xt_lo_made", "glu_made", "lin_made", "u_half", "sig_made",
                  "hid_made"))
        hid_t_ps, hid_hi_made, hid_lo_made, scattered, slot_parts = map(
            sem, ("hid_t_ps", "hid_hi_made", "hid_lo_made", "scattered", "slot_parts"))
        moe_over, acc_loaded, fin_ssq, fin_mean, fin_rms, fin_made, pos_shifted = map(
            sem, ("moe_over", "acc_loaded", "fin_ssq", "fin_mean", "fin_rms", "fin_made",
                  "pos_shifted"))
        h_mean, y_made_half = map(sem, ("h_mean", "y_made_half"))
        fin_loaded = [sem(f"fin_loaded{t}") for t in range(TT)]

        block = ctx.enter_context(nc.Block())

        def silu_tiles(c):
            return (2 * c, 2 * c + 1)

        def router_act(act):
            A_ = nc.scalar.activation
            act.wait_ge(h_made, 2 * N_OUT)
            for t in range(TT):
                if t >= 2:
                    act.wait_ge(h_ssq, t - 1)
                A_(u2[t % 2][:, :], h[:, t, :], ACT.Square, accum_out=ssq2[:, t:t + 1]
                   ).then_inc(h_ssq, 1)
            act.wait_ge(b1_loaded, 32)
            A_(b1_hl[:, :], b1_raw[:, :], ACT.Copy).then_inc(b1_hi_done, 1)
            for t in range(TT):
                act.wait_ge(u_t_ps, t + 1)
                if t >= 2:
                    act.wait_ge(logit_ps, t - 1)
                for i in range(2):
                    A_(u2_t[t % 2][:, 4 * i:4 * i + 4, :].rearrange("p k t -> p (k t)"),
                       bank[2 * (t % 2) + i], ACT.Copy).then_inc(u_t_made, 1)
            act.wait_ge(top_made, 1)
            A_(gexp[:, :], gexp[:, :], ACT.Exp).then_inc(top_exp, 1)

        def router_dve(dve, step):
            V = nc.vector
            dve.wait_ge(h_ssq, TT)
            V.tensor_scalar(rms2[:, :], ssq2[:, :], 1.0 / D, EPS, ALU.mult, ALU.add).then_inc(h_mean, 1)
            dve.wait_ge(router_loaded, 48)
            dve.wait_ge(h_rms, 1)
            for t in range(TT):
                if t >= 2:
                    dve.wait_ge(u_stored[t % 2], 16 * (t // 2))
                    dve.wait_ge(u_t_ps, t - 1)
                V.scalar_tensor_tensor(u2[t % 2][:, :], h[:, t, :], rms2[:, t:t + 1], ffn_g[:, :],
                                       ALU.mult, ALU.mult).then_inc(u_made, 1)
            dve.wait_ge(b1_hi_done, 1)
            V.tensor_tensor(b1_hl[E:2 * E, :], b1_raw[E:2 * E, :], b1_hl[E:2 * E, :].bitcast(F32),
                            ALU.subtract).then_inc(b1_lo_done, 1)
            dve.wait_ge(logit_ps, TT)
            t3 = lambda a, w: a.rearrange("p (t e) -> p t e", t=TT)
            step(V.tensor_tensor(t3(logits[:, :], E), bank[4][:, 0:TT * E].rearrange(
                "p (t e) -> p t e", t=TT), v["b_router"].rearrange("p (o e) -> p o e", o=1)
                .to_broadcast([P, TT, E]), ALU.add))
            for t in range(TT):
                lg = logits[:, E * t:E * t + E]
                step(V.max(out=top[:, 8 * t:8 * t + 8], in_=lg))
                step(V.max_index(out=top_idx[:, 8 * t:8 * t + 8], in_max=top[:, 8 * t:8 * t + 8],
                                 in_values=lg))
            top3 = top[:, :].rearrange("p (t j) -> p t j", t=TT)
            g3 = lambda a: a[:, :].rearrange("p (t j) -> p t j", t=TT)
            V.tensor_tensor(g3(gexp), top3[:, :, 0:TOPK], top3[:, :, 0:1].to_broadcast([P, TT, TOPK]),
                            ALU.subtract).then_inc(top_made, 1)
            step(V.tensor_copy(top_f[:, :], top_idx[:, :]))
            dve.wait_ge(top_exp, 1)
            step(V.tensor_reduce(gsum[:, :], g3(gexp), AX.X, ALU.add))
            step(V.reciprocal(gsum[:, :], gsum[:, :]))
            step(V.tensor_tensor(g3(gate), g3(gexp), gsum[:, :].rearrange("p (t o) -> p t o", o=1)
                                 .to_broadcast([P, TT, TOPK]), ALU.mult))
            ids = const["experts"].rearrange("p (o e) -> p o e", o=1).to_broadcast([P, TT, E])
            idx3 = g3(top_f)
            for j in range(TOPK):
                pk = pick if j else mask
                gk = gpick if j else gates
                step(V.tensor_tensor(g3(pk), ids, idx3[:, :, j:j + 1].to_broadcast([P, TT, E]),
                                     ALU.is_equal))
                step(V.tensor_tensor(g3(gk), g3(pk), g3(gate)[:, :, j:j + 1]
                                     .to_broadcast([P, TT, E]), ALU.mult))
                if j:
                    step(V.tensor_tensor(gates[:, :], gates[:, :], gpick[:, :], ALU.add))
                    ins = V.tensor_tensor(mask[:, :], mask[:, :], pick[:, :], ALU.add)
                    if j < TOPK - 1:
                        step(ins)
                    else:
                        ins.then_inc(mask_made, 1)
            dve.wait_ge(pos_ps, 1)
            step(V.scalar_tensor_tensor(pos[:, :, :].rearrange("p t e -> p (t e)"),
                                        bank[5][:, 0:TT * E], 1.0, mask[:, :], ALU.add, ALU.mult))
            step(V.tensor_scalar(pos[:, :, :], pos[:, :, :], -1.0, None, ALU.add))
            dve.wait_ge(rhs_filled, 4)
            V.tensor_copy(slot_rhs[:, :, :, 1], g3(gates)).then_inc(pos_made, 1)
            step(V.tensor_reduce(n_max[:, :], bank[5][:, TT * E:TT * E + E], AX.X, ALU.max))
            V.tensor_copy(n_max_u[:, :], n_max[:, :]).then_inc(count_made, 1)
            dve.wait_ge(gates_t_ps, 1)
            V.tensor_copy(gates_t[:, :, :].rearrange("e t q -> e (t q)"), bank[6][0:E, :]
                          ).then_inc(gates_t_made, 1)

        def router_pe(pe, three):
            MM = nc.tensor.matmul
            pe.wait_ge(h_made, 2 * N_OUT)
            pe.wait_ge(router_loaded, 48)

            def turn(t):
                pe.wait_ge(u_made, t + 1)
                if t >= 2:
                    pe.wait_ge(u_t_made, 2 * (t - 1))
                for k in range(DK):
                    ins = nc.tensor.transpose(bank[2 * (t % 2) + k // 4][:, P * (k % 4):P * (k % 4) + P],
                                              u2[t % 2][:, P * k:P * k + P], ident)
                ins.then_inc(u_t_ps, 1)

            turn(0)
            for t in range(TT):
                if t + 1 < TT:
                    turn(t + 1)
                pe.wait_ge(u_t_made, 2 * (t + 1))
                for k in range(DK):
                    ins = MM(bank[4][:, E * t:E * t + E], u2_t[t % 2][:, k, :], wr[:, k, :],
                             start=(k == 0), stop=(k == DK - 1))
                ins.then_inc(logit_ps, 1)
            pe.wait_ge(mask_made, 1)
            mk = lambda t: mask[:, E * t:E * t + E]
            for t in range(TT):
                MM(bank[5][:, E * t:E * t + E], const["strict"], mk(t), start=True, stop=(t == 0))
                for s in range(t):
                    MM(bank[5][:, E * t:E * t + E], const["ones"], mk(s), start=False,
                       stop=(s == t - 1))
            for s in range(TT):
                ins = MM(bank[5][:, TT * E:TT * E + E], const["ones"], mk(s), start=(s == 0),
                         stop=(s == TT - 1))
            ins.then_inc(pos_ps, 1)
            for t in range(TT):
                ins = nc.tensor.transpose(bank[6][0:E, P * t:P * t + P], gates[:, E * t:E * t + E], ident)
            ins.then_inc(gates_t_ps, 1)

        LEAD = N_IN + N_OUT
        IT = LEAD + 4
        PRO_USES = [(N_PRO - s + PRO_SLOTS - 1) // PRO_SLOTS for s in range(PRO_SLOTS)] + [0] * 3
        PAIRS = E // 2
        GLU, LINEAR = (0, 2), (1, 3)
        Y0, HT, XT = 4, 6, 7

        def later(g):
            return not isinstance(g, int) or g > 0

        def chunk_slot(j):
            place = (4 + j) % PER_EXPERT
            return EXPERT_SLOT[place], PRO_USES[EXPERT_SLOT[place]] + (4 + j) // PER_EXPERT, (IT + j) % SPLITS

        def high_of(act, ringslot, loads, count, parts):
            act.wait_ge(w_loaded[ringslot], loads)
            act.wait_ge(chunk_used, count - SPLITS)
            nc.scalar.activation(w_hi[parts][:, :], ring[ringslot][:, :], ACT.Copy).then_inc(hi_done, 1)

        def low_of(dve, ringslot, count, parts):
            dve.wait_ge(hi_done, count)
            dve.wait_ge(chunk_used, count - SPLITS)
            nc.vector.tensor_tensor(w_lo[parts][:, :], ring[ringslot][:, :],
                                    w_hi[parts][:, :].bitcast(F32), ALU.subtract).then_inc(lo_done, 1)

        def moe_sync(sp):
            for t in range(TT):
                sp.wait_ge(acc_made, 2 * t + 2)
                sp.dma_start(acc_dram[t * P:(t + 1) * P, :], h[:, t, :]).then_inc(acc_stored, 16)
            sp.dma_start(acc_dram[T:T + P, :], h[:, 0, :]).then_inc(acc_stored, 16)
            sp.wait_ge(acc_stored, 16 * (TT + 1))
            for i in range(2):
                sp.wait_ge(u_stored[i], 16 * TT // 2)
            for m in range(PRO_SLOTS, SLOTS):
                sp.dma_start(ring[EXPERT_SLOT[m]][:, :], stream[N_PRO + m, :, :]
                             ).then_inc(w_loaded[EXPERT_SLOT[m]], 16)

            def rounds(first, base):
                with sp.Fori(first, E) as r:
                    for m in range(PER_EXPERT):
                        slot = EXPERT_SLOT[m]
                        sp.wait_ge(lo_done, (r + base) * PER_EXPERT + (LEAD - PER_EXPERT + m + 1))
                        sp.dma_start(ring[slot][:, :], stream[bass.ds(r * PER_EXPERT + (N_PRO + m), 1),
                                                              :, :]
                                     .rearrange("o p c -> (o p) c")).then_inc(w_loaded[slot], 16)

            rounds(1, 0)
            sp.wait_ge(count_made, 1)
            most = sp.value_load(n_max_u[0:1, 0:1], min_val=0, max_val=T)
            with sp.Fori(1, TT) as b:
                with sp.If(most > b * P):
                    rounds(0, b * E)
            sp.wait_ge(moe_over, 1)
            sp.dma_start(fin_g[:, :], norm_final_g.partition_broadcast(P)).then_inc(acc_loaded, 16)
            for t in range(TT):
                sp.dma_start(fin[t][:, :], acc_dram[t * P:(t + 1) * P, :]).then_inc(fin_loaded[t], 16)
            for t in range(TT):
                sp.wait_ge(fin_made, t + 1)
                sp.dma_start(out[t * P:(t + 1) * P, :], fin[t][:, :]).then_inc(out_stored, 16)
            sp.wait_ge(out_stored, 16 * TT)

        def moe_pool(pool):
            G = nc.gpsimd
            pool.wait_ge(h_mean, 1)
            G.tensor_tensor(rms2[:, :], rms2[:, :], power[:, 0:TT], ALU.pow).then_inc(h_rms, 1)

            def gather(e, g):
                pool.wait_ge(slot_info, g + 1)
                if e >= 2:
                    pool.wait_ge(xt_ps, 2 * (g - 1))
                G.indirect_dma_start(
                    out=xe[e % 2][:, :], out_offset=None, in_=u_dram[:, :],
                    in_offset=bass.IndirectOffsetOnAxis(ap=slot_token[:, e:e + 1], axis=0),
                    bounds_check=T - 1).then_inc(xe_loaded[e % 2], 16)

            def scatter(e, g):
                pool.wait_ge(y_made_half, 2 * g + 2)
                if g:
                    pool.wait_ge(scattered, 16 * g)
                G.indirect_dma_start(
                    out=acc_dram[:, :],
                    out_offset=bass.IndirectOffsetOnAxis(ap=slot_row[:, e:e + 1], axis=0),
                    in_=y_sb[e % 2][:, :], in_offset=None, bounds_check=T + P - 1,
                    compute_op=ALU.add).then_inc(scattered, 16)

            def a_pass(base):
                gather(0, base)
                gather(1, base + 1)
                if base == 0:
                    pool.wait_ge(acc_stored, 16 * (TT + 1))
                for e in range(E):
                    if e + 2 < E:
                        gather(e + 2, base + e + 2)
                    scatter(e, base + e)
                pool.wait_ge(scattered, 16 * (base + E))

            for i in range(2):
                pool.wait_ge(u_stored[i], 16 * TT // 2)
            a_pass(0)
            pool.wait_ge(count_made, 1)
            most = pool.value_load(n_max_u[0:1, 0:1], min_val=0, max_val=T)
            for b in range(1, TT):
                with pool.If(most > b * P):
                    a_pass(b * E)
            G.memset(power[:, :], -0.5).then_inc(moe_over, 1)
            for t in range(TT):
                pool.wait_ge(fin_mean, t + 1)
                G.tensor_tensor(fin_rms_t[:, t:t + 1], fin_rms_t[:, t:t + 1], power[:, 0:1], ALU.pow
                                ).then_inc(fin_rms, 1)

        def moe_act(act):
            A_ = nc.scalar.activation

            def high(j, g):
                slot, uses, parts = chunk_slot(j)
                high_of(act, slot, g * 16 + 16 * (uses + 1), g * PER_EXPERT + (IT + j + 1), parts)

            def x_part(g, par, i):
                act.wait_ge(xt_ps, g * 2 + i + 1)
                A_(xe_hi[par][:, 4 * i:4 * i + 4, :].rearrange("p k s -> p (k s)"), bank[XT], ACT.Copy
                   ).then_inc(xt_hi_made, 1)

            def sigmoid(g, half):
                act.wait_ge(glu_made, g * 2 + half + 1)
                if later(g) or half:
                    act.wait_ge(hid_made, g * 2 + half)
                A_(sig[:, :], glu[:, :], ACT.Sigmoid, scale=1.702).then_inc(sig_made, 1)

            def hid_part(g, half):
                act.wait_ge(hid_t_ps, g * 2 + half + 1)
                A_(hid_hi[half][:, :, :].rearrange("p f s -> p (f s)"), bank[HT], ACT.Copy
                   ).then_inc(hid_hi_made, 1)

            def outputs(e, g, par, count):
                act.wait_ge(chunk_used, count)
                if later(g):
                    act.wait_ge(scattered, 16 * g)
                for i in range(2):
                    A_(y_sb[par][:, 512 * i:512 * i + 512], bank[Y0 + i], ACT.Copy,
                       scale=slot_gate[:, bass.ds(e, 1)]).then_inc(y_made_half, 1)

            def iteration(e, g, par, last):
                high(3, g)
                hid_part(g, 0)
                high(4, g)
                high(5, g)
                if not last:
                    x_part(g + 1, 1 - par, 0)
                high(6, g)
                sigmoid(g, 1)
                if not last:
                    x_part(g + 1, 1 - par, 1)
                high(7, g)
                if not last:
                    high(8, g)
                    high(9, g)
                hid_part(g, 1)
                if not last:
                    high(10, g)
                    high(11, g)
                    high(12, g)
                    sigmoid(g + 1, 0)
                    high(13, g)
                    high(14, g)
                outputs(e, g, par, g * PER_EXPERT + (IT + (8 if last else 12)))

            def a_pass(base, first):
                for j in range(4):
                    c = LEAD + j
                    high_of(act, EXPERT_SLOT[j], base * 16 + 16 * (PRO_USES[EXPERT_SLOT[j]] + 1),
                            base * PER_EXPERT + (c + 1), c % SPLITS)
                    if j == 2:
                        x_part(base, 0, 0)
                        x_part(base, 0, 1)
                high(0, base)
                sigmoid(base, 0)
                high(1, base)
                high(2, base)
                for par in range(2 * first):
                    iteration(par, par, par, False)
                with act.Fori(first, PAIRS - 1) as i:
                    for par in range(2):
                        iteration(i * 2 + par, i * 2 + (base + par), par, False)
                for par in range(2):
                    iteration(E - 2 + par, base + (E - 2 + par), par, par == 1)

            a_pass(0, 1)
            act.wait_ge(count_made, 1)
            most = act.value_load(n_max_u[0:1, 0:1], min_val=0, max_val=T)
            with act.Fori(1, TT) as b:
                with act.If(most > b * P):
                    a_pass(b * E, 0)
            for t in range(TT):
                act.wait_ge(fin_loaded[t], 16)
                if t:
                    act.wait_ge(fin_ssq, t)
                A_(fin_junk[:, :], fin[t][:, :], ACT.Square, accum_out=fin_ssq_t[:, t:t + 1]
                   ).then_inc(fin_ssq, 1)

        def moe_dve(dve):
            V = nc.vector
            f = lambda a: a.bitcast(F32)

            def low(j, g):
                slot, _, parts = chunk_slot(j)
                low_of(dve, slot, g * PER_EXPERT + (IT + j + 1), parts)

            def slot_masks(e, g):
                if later(g):
                    dve.wait_ge(slot_ps, g)
                for t in range(TT):
                    ins = V.tensor_scalar(onehot[:, t, :], const["slots"], pos[:, t, bass.ds(e, 1)],
                                          None, ALU.is_equal)
                ins.then_inc(onehot_made, 1)

            def select(e, par):
                V.tensor_copy(sel[par][:, :], const["rows2e"][0:2 * E, bass.ds(e, 1)]
                              .to_broadcast([2 * E, P])).then_inc(sel_made, 1)

            def slot_scalars(e, g):
                dve.wait_ge(slot_ps, g + 1)
                V.tensor_copy(slot_token[:, bass.ds(e, 1)], bank[XT][:, 0:1]).then_inc(slot_parts, 1)
                V.tensor_copy(slot_gate[:, bass.ds(e, 1)], bank[XT][:, 1:2]).then_inc(slot_parts, 1)
                V.tensor_scalar(valid[:, :], bank[XT][:, 2:3], -1.0, 1.0, ALU.mult, ALU.add
                                ).then_inc(slot_parts, 1)
                dve.wait_ge(slot_parts, g * 3 + 3)
                V.scalar_tensor_tensor(slot_row[:, bass.ds(e, 1)], const["trash"], valid[:, 0:1],
                                       bank[XT][:, 0:1], ALU.mult, ALU.add).then_inc(slot_info, 1)

            def x_part(g, par, i):
                dve.wait_ge(xt_hi_made, g * 2 + i + 1)
                V.tensor_tensor(xe_lo[par][:, 4 * i:4 * i + 4, :].rearrange("p k s -> p (k s)"),
                                bank[XT], f(xe_hi[par][:, 4 * i:4 * i + 4, :]
                                            .rearrange("p k s -> p (k s)")), ALU.subtract
                                ).then_inc(xt_lo_made, 1)

            def clamp(g, half, count):
                dve.wait_ge(chunk_used, count)
                if later(g) or half:
                    dve.wait_ge(hid_t_ps, g * 2 + half)
                V.tensor_scalar(glu[:, :], bank[GLU[half]], 7.0, None, ALU.min).then_inc(glu_made, 1)
                V.tensor_scalar(lin[:, :], bank[LINEAR[half]], 7.0, -7.0, ALU.min, ALU.max
                                ).then_inc(lin_made, 1)

            def hidden(g, half):
                dve.wait_ge(lin_made, g * 2 + half + 1)
                V.scalar_tensor_tensor(lin[:, :], lin[:, :], 1.0, glu[:, :], ALU.add, ALU.mult
                                       ).then_inc(u_half, 1)
                dve.wait_ge(u_half, g * 2 + half + 1)
                dve.wait_ge(sig_made, g * 2 + half + 1)
                V.tensor_tensor(lin[:, :], lin[:, :], sig[:, :], ALU.mult).then_inc(hid_made, 1)

            def hid_part(g, half):
                dve.wait_ge(hid_hi_made, g * 2 + half + 1)
                V.tensor_tensor(hid_lo[half][:, :, :].rearrange("p f s -> p (f s)"), bank[HT],
                                f(hid_hi[half][:, :, :].rearrange("p f s -> p (f s)")), ALU.subtract
                                ).then_inc(hid_lo_made, 1)

            def iteration(e, g, par, last, far):
                low(3, g)
                hid_part(g, 0)
                if far:
                    slot_masks(e + 2, g + 2)
                low(4, g)
                if not last:
                    select(e + 1, 1 - par)
                low(5, g)
                if not last:
                    x_part(g + 1, 1 - par, 0)
                clamp(g, 1, g * PER_EXPERT + (IT + 4))
                low(6, g)
                if not last:
                    x_part(g + 1, 1 - par, 1)
                hidden(g, 1)
                low(7, g)
                if not last:
                    low(8, g)
                    if far:
                        slot_scalars(e + 2, g + 2)
                    low(9, g)
                hid_part(g, 1)
                if not last:
                    low(10, g)
                    low(11, g)
                    clamp(g + 1, 0, g * PER_EXPERT + (IT + 10))
                    low(12, g)
                    hidden(g + 1, 0)
                    low(13, g)
                    low(14, g)

            def constants():
                dve.wait_ge(gates_t_made, 1)
                for i in range(2 * TT):
                    t, half = i // 2, i % 2
                    dve.wait_ge(b2_ps, i + 1)
                    dst = h[:, t, 512 * half:512 * half + 512]
                    V.tensor_tensor(dst, dst, bank[i % 4], ALU.add).then_inc(acc_made, 1)

            def a_pass(base, first):
                for e in range(2):
                    slot_masks(e, base + e)
                    slot_scalars(e, base + e)
                if first:
                    constants()
                select(0, 0)
                for j in range(4):
                    c = LEAD + j
                    low_of(dve, EXPERT_SLOT[j], base * PER_EXPERT + (c + 1), c % SPLITS)
                    if j == 2:
                        x_part(base, 0, 0)
                        x_part(base, 0, 1)
                clamp(base, 0, base * PER_EXPERT + (LEAD + 4))
                low(0, base)
                hidden(base, 0)
                low(1, base)
                low(2, base)
                for par in range(2 * first):
                    iteration(par, par, par, False, True)
                with dve.Fori(first, PAIRS - 1) as i:
                    for par in range(2):
                        iteration(i * 2 + par, i * 2 + (base + par), par, False, True)
                for par in range(2):
                    iteration(E - 2 + par, base + (E - 2 + par), par, par == 1, False)

            dve.wait_ge(pos_made, 1)
            a_pass(0, 1)
            dve.wait_ge(count_made, 1)
            most = dve.value_load(n_max_u[0:1, 0:1], min_val=0, max_val=T)
            with dve.Fori(1, TT) as b:
                with dve.If(most > b * P):
                    V.tensor_scalar(pos[:, :, :], pos[:, :, :], -float(P), None, ALU.add
                                    ).then_inc(pos_shifted, 1)
                    dve.wait_ge(pos_shifted, b)
                    a_pass(b * E, 0)
            dve.wait_ge(acc_loaded, 16)
            for t in range(TT):
                dve.wait_ge(fin_ssq, t + 1)
                V.tensor_scalar(fin_rms_t[:, t:t + 1], fin_ssq_t[:, t:t + 1], 1.0 / D, EPS, ALU.mult,
                                ALU.add).then_inc(fin_mean, 1)
                dve.wait_ge(fin_rms, t + 1)
                V.scalar_tensor_tensor(fin[t][:, :], fin[t][:, :], fin_rms_t[:, t:t + 1], fin_g[:, :],
                                       ALU.mult, ALU.mult).then_inc(fin_made, 1)

        def moe_pe(pe):
            MM = nc.tensor.matmul

            def products(count, parts, outs, xh, xl, k0, width, first, last):
                wh = w_hi[parts][:, :].rearrange("p (k c) -> p k c", k=2)
                wl = w_lo[parts][:, :].rearrange("p (k c) -> p k c", k=2)
                pe.wait_ge(hi_done, count)
                for i in range(2):
                    for n in range(2):
                        cols = slice(512 * n, 512 * n + 512)
                        MM(outs[n], xh[:, k0 + i, :], wh[:, i, cols], start=(first and i == 0), stop=False)
                        MM(outs[n], xl[:, k0 + i, :], wh[:, i, cols], start=False, stop=False)
                pe.wait_ge(lo_done, count)
                for i in range(2):
                    for n in range(2):
                        cols = slice(512 * n, 512 * n + 512)
                        ins = MM(outs[n], xh[:, k0 + i, :], wl[:, i, cols], start=False,
                                 stop=(last and i == 1))
                ins.then_inc(chunk_used, 1)

            def w1_start(g, half, par):
                pe.wait_ge(sel_made, g + 1)
                for n, b in enumerate((GLU[half], LINEAR[half])):
                    c0 = D * n + 512 * half
                    MM(bank[b], sel[par][:, :], b1_hl[:, c0:c0 + 512], start=True, stop=False)

            def w1_chunk(count, parts, half, par, k0):
                products(count, parts, (bank[GLU[half]], bank[LINEAR[half]]), xe_hi[par], xe_lo[par],
                         k0, 512, False, k0 == DK - 2)

            def w2_chunk(count, parts, half, f0):
                products(count, parts, (bank[Y0], bank[Y0 + 1]), hid_hi[half], hid_lo[half], f0, 512,
                         half == 0 and f0 == 0, half == 1 and f0 == 2)

            def slots(e, g):
                pe.wait_ge(onehot_made, g + 1)
                for t in range(TT):
                    ins = MM(bank[XT][:, 0:4], onehot[:, t, :],
                             slot_rhs[:, t, bass.ds(e, 1), :].rearrange("p o j -> p (o j)"),
                             start=(t == 0), stop=(t == TT - 1))
                ins.then_inc(slot_ps, 1)

            def turn_x(g, pair, par, i):
                if i == 0:
                    pe.wait_ge(xe_loaded[par], pair * 16 + 16)
                else:
                    pe.wait_ge(xt_lo_made, g * 2 + 1)
                for k in range(4):
                    ins = nc.tensor.transpose(bank[XT][:, P * k:P * k + P],
                                              xe[par][:, P * (4 * i + k):P * (4 * i + k) + P], ident)
                ins.then_inc(xt_ps, 1)

            def turn_hid(g, half):
                pe.wait_ge(hid_made, g * 2 + half + 1)
                for k in range(4):
                    ins = nc.tensor.transpose(bank[HT][:, P * k:P * k + P], lin[:, P * k:P * k + P],
                                              ident)
                ins.then_inc(hid_t_ps, 1)

            def iteration(e, g, pair, par, last, far):
                def count(j):
                    return g * PER_EXPERT + (IT + j + 1)

                parts = lambda j: chunk_slot(j)[2]
                if later(g):
                    pe.wait_ge(lin_made, g * 2)
                w1_start(g, 1, par)
                for j in range(4):
                    w1_chunk(count(j), parts(j), 1, par, 2 * j)
                    if j == 1:
                        turn_hid(g, 0)
                if not last:
                    pe.wait_ge(slot_info, g + 2)
                    turn_x(g + 1, pair + par, 1 - par, 0)
                if later(g):
                    pe.wait_ge(y_made_half, g * 2)
                pe.wait_ge(hid_lo_made, g * 2 + 1)
                w2_chunk(count(4), parts(4), 0, 0)
                if not last:
                    turn_x(g + 1, pair + par, 1 - par, 1)
                w2_chunk(count(5), parts(5), 0, 2)
                j = 6
                if not last:
                    pe.wait_ge(lin_made, g * 2 + 1)
                    pe.wait_ge(xt_lo_made, g * 2 + 4)
                    w1_start(g + 1, 0, 1 - par)
                    for j in range(6, 10):
                        w1_chunk(count(j), parts(j), 0, 1 - par, 2 * (j - 6))
                        if j == 6 and far:
                            slots(e + 2, g + 2)
                        if j == 7:
                            turn_hid(g, 1)
                    j = 10
                else:
                    turn_hid(g, 1)
                pe.wait_ge(hid_lo_made, g * 2 + 2)
                w2_chunk(count(j), parts(j), 1, 0)
                w2_chunk(count(j + 1), parts(j + 1), 1, 2)

            def constants():
                pe.wait_ge(gates_t_made, 1)
                for i in range(2 * TT):
                    t, half = i // 2, i % 2
                    if i >= 4:
                        pe.wait_ge(acc_made, i - 3)
                    MM(bank[i % 4], gates_t[:, t, :], b2_sb[:, 512 * half:512 * half + 512],
                       start=True, stop=True).then_inc(b2_ps, 1)
                pe.wait_ge(acc_made, 2 * TT)

            def a_pass(base, pair0, first):
                slots(0, base)
                pe.wait_ge(slot_info, base + 1)
                slots(1, base + 1)
                pe.wait_ge(slot_info, base + 2)
                if first:
                    constants()
                    pe.wait_ge(b1_lo_done, 1)
                turn_x(base, pair0, 0, 0)
                turn_x(base, pair0, 0, 1)
                if not first:
                    pe.wait_ge(lin_made, base * 2)
                pe.wait_ge(xt_lo_made, base * 2 + 2)
                w1_start(base, 0, 0)
                for j in range(4):
                    w1_chunk(base * PER_EXPERT + (LEAD + j + 1), (LEAD + j) % SPLITS, 0, 0, 2 * j)
                for par in range(2 * first):
                    iteration(par, par, 0, par, False, True)
                with pe.Fori(first, PAIRS - 1) as i:
                    for par in range(2):
                        iteration(i * 2 + par, i * 2 + (base + par), i + pair0, par, False, True)
                for par in range(2):
                    iteration(E - 2 + par, base + (E - 2 + par), pair0 + (PAIRS - 1), par, par == 1,
                              False)

            pe.wait_ge(pos_made, 1)
            a_pass(0, 0, 1)
            pe.wait_ge(count_made, 1)
            most = pe.value_load(n_max_u[0:1, 0:1], min_val=0, max_val=T)
            with pe.Fori(1, TT) as b:
                with pe.If(most > b * P):
                    a_pass(b * E, b * PAIRS, 0)

        @block.sync
        def _(sp):
            def load_chunk(slot, n):
                sp.dma_start(ring[slot][:, :], stream[n, :, :]).then_inc(w_loaded[slot], 16)

            sp.dma_start(vec[:, :], vectors[:, :]).then_inc(vec_loaded, 16)
            for n in range(N_X + 1):
                load_chunk(n, n)
            sp.dma_start(main[:, :], consts[:, 0:main_w]).then_inc(const_loaded, 16)
            sp.dma_start(wdt[:, :, :], w_dt[:, :, :]).then_inc(const_loaded, 16)
            bw = main_w + 2 * P
            sp.dma_start(band[:, 0:FW], consts[0:BUCKETS + 1, bw:bw + FW]).then_inc(const_loaded, 16)
            sp.dma_start(rel[0:BUCKETS, :], rel_bias[:, :]).then_inc(const_loaded, 16)
            sp.dma_start(rel[BUCKETS:BUCKETS + 1, :],
                         consts[0:1, bw + FW:bw + FW + HEADS]).then_inc(const_loaded, 16)
            for n in range(N_X + 1, PRO_SLOTS):
                load_chunk(n, n)
            sp.wait_ge(band_made, 1)
            sp.dma_start(bass.AP(band_dram, 0, [[FW, HEADS], [HEADS * FW, P], [1, FW]]),
                         band_rows[:, 0:FW].rearrange("h (o f) -> h o f", o=1)
                         .to_broadcast([HEADS, P, FW])).then_inc(band_stored, 16)
            for n in range(PRO_SLOTS, N_PRO):
                if n < PRO_SLOTS + N_X:
                    sp.wait_ge(xg_lo_done, 4 * (n - PRO_SLOTS + 1))
                    sp.wait_ge(sq_done, n - PRO_SLOTS + 1)
                else:
                    sp.wait_ge(lo_done, n - PRO_SLOTS - N_X + 1)
                load_chunk(n % PRO_SLOTS, n)
            for m in range(5):
                sp.wait_ge(lo_done, 5 + m)
                load_chunk(EXPERT_SLOT[m], N_PRO + m)
            sp.wait_ge(chunk_used, N_IN)
            sp.dma_start(incl[:, :], consts[:, main_w:main_w + P]).then_inc(scan_consts_loaded, 16)
            sp.dma_start(negmask[:, :], consts[:, main_w + P:main_w + 2 * P]
                         ).then_inc(scan_consts_loaded, 16)
            sp.wait_ge(silu_done, 8)
            sp.wait_ge(band_stored, 16)
            sp.dma_start(bias[:, :, :], bass.AP(band_dram, P - 1, [[HEADS * FW - 1, P], [FW, HEADS],
                                                                   [1, 2 * P]])
                         ).then_inc(bias_loaded, 16)
            sp.dma_start(h[:, :, :], x.rearrange("(t p) d -> p t d", p=P)).then_inc(h_loaded, 16)
            sp.wait_ge(mix_ps, 1)
            sp.dma_start(ffn_g[:, :], norm_ffn_g.partition_broadcast(P)).then_inc(router_loaded, 16)
            sp.dma_start(wr[:, :, :], w_router.rearrange("(k p) e -> p k e", p=P)
                         ).then_inc(router_loaded, 16)
            sp.dma_start(b2_sb[:, :], b2[:, :]).then_inc(router_loaded, 16)
            for m in range(5, PRO_SLOTS):
                sp.wait_ge(lo_done, 5 + m)
                load_chunk(EXPERT_SLOT[m], N_PRO + m)
            sp.wait_ge(chunk_used, N_IN + N_OUT)
            sp.dma_start(b1_raw[0:E, :], b1[:, :]).then_inc(b1_loaded, 16)
            sp.dma_start(b1_raw[E:2 * E, :], b1[:, :]).then_inc(b1_loaded, 16)
            for t in range(TT):
                sp.wait_ge(u_made, t + 1)
                sp.dma_start(u_dram[t * P:(t + 1) * P, :], u2[t % 2][:, :]).then_inc(u_stored[t % 2], 16)
            moe_sync(sp)

        @block.gpsimd
        def _(pool):
            nc.gpsimd.memset(conv_in[:, :, 0:4], 0.0).then_inc(pads_made, 1)
            nc.gpsimd.memset(k_t[:, 0:P], 0.0).then_inc(pads_made, 1)
            nc.gpsimd.memset(v_tok[:, 0, :], 0.0).then_inc(pads_made, 1)
            nc.gpsimd.memset(slot_rhs[:, :, :, 2], 1.0).then_inc(rhs_filled, 1)
            nc.gpsimd.memset(slot_rhs[:, :, :, 3], 0.0).then_inc(rhs_filled, 1)
            pool.wait_ge(const_loaded, 80)
            nc.gpsimd.tensor_copy(slot_rhs[:, :, :, 0], const["tokens"].rearrange("p (t o) -> p t o", o=1)
                                  .to_broadcast([P, TT, E])).then_inc(rhs_filled, 1)
            nc.gpsimd.memset(power[:, :], -0.5).then_inc(rhs_filled, 1)

            def inverse_root(c):
                pool.wait_ge(mean_made, c + 1)
                pool.wait_ge(rhs_filled, 4)
                nc.gpsimd.tensor_tensor(rms[:, 2 * c:2 * c + 2], rms[:, 2 * c:2 * c + 2],
                                        power[:, 0:2], ALU.pow).then_inc(rms_made, 1)

            pool.wait_ge(cum_exp, 3)
            for c in range(TT):
                pool.wait_ge(tok_made, 2 * c + 1)
                if c:
                    pool.wait_ge(y_ps, c)
                    pool.wait_ge(y_read, c)
                xt = x_toks[c % 2][:, :].rearrange("p (h d) -> p h d", h=HEADS)

                def per_head(a):
                    return a.rearrange("p (h o) -> p h o", o=1).to_broadcast([P, HEADS, HD])

                o3 = lambda a: a[:, :].rearrange("p (h d) -> p h d", h=HEADS)
                nc.gpsimd.tensor_tensor(o3(xdt), xt, per_head(dt[:, 8 * c:8 * c + 8]), ALU.mult
                                        ).then_inc(xs_made, 1)
                pool.wait_ge(xs_made, 3 * c + 1)
                nc.gpsimd.tensor_tensor(o3(xdd), o3(xdt), per_head(dend[:, 8 * c:8 * c + 8]),
                                        ALU.mult).then_inc(xs_made, 1)
                nc.gpsimd.tensor_tensor(o3(xskip), xt, per_head(v["d_skip"]), ALU.mult
                                        ).then_inc(xs_made, 1)
                if c:
                    inverse_root(c - 1)
            inverse_root(TT - 1)
            moe_pool(pool)

        @block.scalar
        def _(act):
            A_ = nc.scalar.activation
            act.wait_ge(vec_loaded, 16)
            for n in range(N_X):
                act.wait_ge(w_loaded[n], 16)
                for j in range(4):
                    k = 4 * n + j
                    A_(xg_hi[:, k, :], ring[n][:, j * T:(j + 1) * T], ACT.Copy,
                       scale=v["norm_mix_g"][:, k:k + 1]).then_inc(xg_hi_done, 1)

            def high(c):
                n = c + N_X
                slot = n % PRO_SLOTS
                act.wait_ge(w_loaded[slot], 16 * (n // PRO_SLOTS + 1))
                if c >= SPLITS:
                    act.wait_ge(chunk_used, c - SPLITS + 1)
                A_(w_hi[c % SPLITS][:, :], ring[slot][:, :], ACT.Copy).then_inc(hi_done, 1)

            def after_proj(c):
                if c < N_XBC:
                    for i in silu_tiles(c):
                        if i == 0:
                            act.wait_ge(band_stored, 16)
                        act.wait_ge(conv_done, i + 1)
                        A_(xbc[:, i, :], conv_acc[:, i % 2, :], ACT.Silu).then_inc(silu_done, 1)
                elif c < N_XBC + N_Z:
                    half = c - N_XBC
                    act.wait_ge(chunk_used, c + 1)
                    act.wait_ge(rstd_tok_made, 1)
                    act.wait_ge(ss_ps, 1)
                    for t in range(TT):
                        b = 2 * (c % 3) + t // 2
                        A_(zs[:, t, 256 * half:256 * half + 256],
                           bank[b][:, 256 * (t % 2):256 * (t % 2) + 256], ACT.Silu,
                           scale=rstd_tok[:, t:t + 1]).then_inc(z_made, 1)
                elif c == N_XBC + N_Z:
                    act.wait_ge(chunk_used, c + 1)
                    for t in range(TT):
                        A_(v_tok[:, t + 1, :], bank[2 * (c % 3) + 1][:, P * t:P * t + P], ACT.Copy,
                           scale=rstd_tok[:, t:t + 1]).then_inc(v_made, 1)

            high(0)
            for n in range(N_X):
                A_(sq[:, 4 * n:4 * n + 4, :].rearrange("p k t -> p (k t)"), ring[n][:, :], ACT.Square
                   ).then_inc(sq_done, 1)
            high(1)
            high(2)
            act.wait_ge(const_loaded, 80)
            A_(wdt_hi[:, :, :], wdt[:, :, :], ACT.Copy).then_inc(wdt_hi_done, 1)
            act.wait_ge(ms_made, 1)
            A_(rstd_row[:, :], rstd_row[:, :], ACT.Sqrt).then_inc(rms_root, 1)
            for c in range(3, N_IN):
                high(c)
                if c <= 6:
                    after_proj(c - 3)
                if c >= 6:
                    after_proj(c - 2)

            act.wait_ge(dt_arg, 1)
            A_(dt_e[:, :], dt_e[:, :], ACT.Exp, scale=-1.0).then_inc(dt_exp, 1)
            A_(a_neg[:, :], v["a_log"], ACT.Exp).then_inc(a_exp, 1)
            act.wait_ge(dt_one, 1)
            A_(dt_l[:, :], dt_u[:, :], ACT.Ln).then_inc(dt_log, 1)
            act.wait_ge(cum_made, 3)
            A_(eacum[:, :], acum[:, :], ACT.Exp).then_inc(cum_exp, 1)
            A_(dtot[:, :], dtot[:, :], ACT.Exp).then_inc(cum_exp, 1)
            A_(dend[:, :], dend[:, :], ACT.Exp).then_inc(cum_exp, 1)

            def exps(a):
                lo = P if a // 4 == 0 else 0
                act.wait_ge(nmax_made, a + 1)
                if a >= 2:
                    act.wait_ge(pt_ps, a - 1)
                for i in range(2):
                    A_(probs[a % 2][:, i, lo:], scores[a % 2][:, i, lo:], ACT.Exp,
                       bias=nmax[:, 2 * a + i:2 * a + i + 1],
                       accum_out=psums[:, 2 * a + i:2 * a + i + 1]).then_inc(exp_made, 1)
                A_(esink[:, 2 * a:2 * a + 2], sinkd[:, 2 * a:2 * a + 2], ACT.Exp).then_inc(exp_made, 1)

            def scan(c, q):
                if q == 0:
                    act.wait_ge(tok_ps, c + 1)
                    if c >= 2:
                        act.wait_ge(xs_made, 3 * (c - 1))
                    A_(x_toks[c % 2][:, :], bank[0][:, :], ACT.Copy).then_inc(tok_made, 1)
                    A_(b_toks[c % 2][:, :, :].rearrange("p g n -> p (g n)"), bank[1][:, 0:256],
                       ACT.Copy).then_inc(tok_made, 1)
                elif q in (1, 2):
                    g = q - 1
                    act.wait_ge(bc_ps, 2 * c + g + 1)
                    if c:
                        act.wait_ge(m_made, 2 * c - 1 + g)
                    for r in range(4):
                        j = 8 * c + 4 * g + r
                        A_(decay[g][:, r, :], bank[2][:, P * r:P * r + P], ACT.Exp,
                           bias=nacum[:, j:j + 1]).then_inc(decay_made, 1)

            def norm(c):
                act.wait_ge(o_read, 4 * c + 4)
                act.wait_ge(y_read, c + 1)
                for i in range(2):
                    if 2 * c + i:
                        act.wait_ge(ssq_made, 2 * c + i)
                    A_(sq_junk[:, :], mix[:, c, 512 * i:512 * i + 512], ACT.Square,
                       accum_out=ssq[:, 2 * c + i:2 * c + i + 1]).then_inc(ssq_made, 1)
                act.wait_ge(rms_made, c + 1)
                for i in range(2):
                    A_(mix[:, c, 512 * i:512 * i + 512], mix[:, c, 512 * i:512 * i + 512], ACT.Copy,
                       scale=rms[:, 2 * c + i:2 * c + i + 1]).then_inc(normed, 1)

            exps(0)
            exps(1)
            for a in range(16):
                c, q = a // 4, a % 4
                act.wait_ge(pt_ps, a + 1)
                if a >= 2:
                    act.wait_ge(o_ps, a - 1)
                lo = 2 if c == 0 else 0
                if c == 0:
                    A_(probs_t[a % 2][:, 2:4, :].rearrange("p a b -> p (a b)"), bank[6][:, 256:512],
                       ACT.Copy).then_inc(pt_made, 1)
                else:
                    A_(probs_t[a % 2][:, :, :].rearrange("p a b -> p (a b)"), bank[6][:, :],
                       ACT.Copy).then_inc(pt_made, 1)
                scan(c, q)
                if a + 2 < 16:
                    exps(a + 2)
                if q == 1 and c:
                    norm(c - 1)
            norm(TT - 1)

            act.wait_ge(mix_ps, 1)
            high(N_IN)
            for k in range(DK):
                act.wait_ge(mix_ps, k + 1)
                A_(mix_hi[:, k, :], bank[k][:, :], ACT.Copy, scale=v["mix_g"][:, k:k + 1]
                   ).then_inc(mix_hi_done, 1)
            for c in range(N_IN + 1, N_IN + N_OUT):
                high(c)
            router_act(act)
            moe_act(act)

        @block.vector
        def _(dve):
            V = nc.vector
            steps = [0]

            def step(ins):
                steps[0] += 1
                ins.then_inc(dve_step, 1)
                dve.wait_ge(dve_step, steps[0])

            f = lambda a: a.bitcast(F32)
            dve.wait_ge(vec_loaded, 16)
            for n in range(N_X):
                for j in range(4):
                    k = 4 * n + j
                    dve.wait_ge(xg_hi_done, k + 1)
                    V.scalar_tensor_tensor(xg_lo[:, k, :], ring[n][:, j * T:(j + 1) * T],
                                           v["norm_mix_g"][:, k:k + 1], f(xg_hi[:, k, :]),
                                           ALU.mult, ALU.subtract).then_inc(xg_lo_done, 1)
            def low(c):
                n = c + N_X
                slot = n % PRO_SLOTS
                dve.wait_ge(hi_done, c + 1)
                if c >= SPLITS:
                    dve.wait_ge(chunk_used, c - SPLITS + 1)
                V.tensor_tensor(w_lo[c % SPLITS][:, :], ring[slot][:, :], f(w_hi[c % SPLITS][:, :]),
                                ALU.subtract).then_inc(lo_done, 1)

            evacs = [0]

            def evac(dst, src):
                V.tensor_tensor(dst, src, rstd_row[:, :], ALU.mult).then_inc(proj_evac, 1)
                evacs[0] += 1

            def after_proj(c):
                b = 2 * (c % 3)
                if c < N_XBC:
                    dve.wait_ge(chunk_used, c + 1)
                    for i, tile in enumerate(silu_tiles(c)):
                        evac(conv_in[:, tile % 2, 3:3 + T], bank[b + i][:, :])
                        dve.wait_ge(proj_evac, evacs[0])
                        if tile >= 2:
                            dve.wait_ge(silu_done, tile - 1)
                        w4 = v["conv_w"][:, 4 * tile:4 * tile + 4]
                        src, dst = conv_in[:, tile % 2, :], conv_acc[:, tile % 2, :]
                        step(V.tensor_scalar(dst, src[:, 0:T], w4[:, 0:1],
                                             v["conv_b"][:, tile:tile + 1], ALU.mult, ALU.add))
                        for j in range(1, 4):
                            ins = V.scalar_tensor_tensor(dst, src[:, j:j + T], w4[:, j:j + 1], dst,
                                                         ALU.mult, ALU.add)
                            if j < 3:
                                step(ins)
                            else:
                                ins.then_inc(conv_done, 1)
                    dve.wait_ge(conv_done, 2 * c + 2)
                elif c == N_XBC + N_Z:
                    dve.wait_ge(chunk_used, c + 1)
                    evac(k_t[:, P:], bank[b][:, :])
                elif c > N_XBC + N_Z:
                    dve.wait_ge(chunk_used, c + 1)
                    dve.wait_ge(dt_t_ps, 1)
                    for i in range(2):
                        evac(q_t[:, 2 * (c - N_XBC - N_Z - 1) + i, :], bank[b + i][:, :])

            low(0)
            low(1)
            dve.wait_ge(band_ps, 1)
            V.tensor_copy(band_rows[:, 0:FW], bank[7][0:HEADS, 0:FW]).then_inc(band_made, 1)
            dve.wait_ge(wdt_hi_done, 1)
            V.tensor_tensor(wdt_lo[:, :, :], wdt[:, :, :], f(wdt_hi[:, :, :]), ALU.subtract
                            ).then_inc(wdt_lo_done, 1)
            low(2)
            dve.wait_ge(ss_ps, 1)
            V.tensor_scalar(rstd_row[:, :], bank[6][:, :], 1.0 / D, EPS, ALU.mult, ALU.add
                            ).then_inc(ms_made, 1)
            dve.wait_ge(rms_root, 1)
            V.reciprocal(rstd_row[:, :], rstd_row[:, :]).then_inc(rstd_made, 1)
            dve.wait_ge(rstd_made, 1)
            dve.wait_ge(pads_made, 3)
            after_proj(0)
            for c in range(3, N_IN):
                low(c)
                if c == 3:
                    dve.wait_ge(rstd_t_ps, 1)
                    V.tensor_copy(rstd_tok[:, :], bank[7][:, :].rearrange("p (t q) -> p t q", t=TT)
                                  [:, :, 0]).then_inc(rstd_tok_made, 1)
                after_proj(c - 2)
                if c == 4:
                    dve.wait_ge(dt_ps, 1)
                    V.tensor_tensor(dt_row[:, :], bank[7][0:HEADS, :], rstd_row[0:HEADS, :], ALU.mult
                                    ).then_inc(dt_row_made, 1)
            after_proj(N_IN - 2)
            after_proj(N_IN - 1)
            dve.wait_ge(proj_evac, evacs[0])

            dve.wait_ge(chunk_used, N_IN)
            row8 = lambda a: a.rearrange("p (o h) -> p o h", o=1).to_broadcast([P, TT, HEADS])
            th = lambda a: a[:, :].rearrange("p (t h) -> p t h", t=TT)
            step(V.tensor_tensor(th(dt_raw), bank[7][:, 0:32].rearrange("p (t h) -> p t h", t=TT),
                                 row8(v["dt_bias"]), ALU.add))
            V.scalar_tensor_tensor(dt_e[:, :], dt_raw[:, :], -1.0, dt_raw[:, :], ALU.mult, ALU.max
                                   ).then_inc(dt_arg, 1)
            dve.wait_ge(dt_exp, 1)
            V.tensor_scalar(dt_u[:, :], dt_e[:, :], 1.0, None, ALU.add).then_inc(dt_one, 1)
            dve.wait_ge(dt_one, 1)
            step(V.tensor_scalar(dt_d[:, :], dt_u[:, :], -1.0, None, ALU.add))
            step(V.tensor_tensor(dt_d[:, :], dt_e[:, :], dt_d[:, :], ALU.subtract))
            step(V.reciprocal(dt[:, :], dt_u[:, :]))
            step(V.tensor_tensor(dt_d[:, :], dt_d[:, :], dt[:, :], ALU.mult))
            dve.wait_ge(dt_log, 1)
            step(V.tensor_tensor(dt_l[:, :], dt_l[:, :], dt_d[:, :], ALU.add))
            step(V.tensor_scalar(dt_d[:, :], dt_raw[:, :], 0.0, None, ALU.max))
            step(V.tensor_tensor(dt[:, :], dt_d[:, :], dt_l[:, :], ALU.add))
            dve.wait_ge(a_exp, 1)
            step(V.tensor_scalar(a_neg[:, :], a_neg[:, :], -1.0, None, ALU.mult))
            V.tensor_tensor(th(adt), th(dt), row8(a_neg[:, :]), ALU.mult).then_inc(adt_made, 1)
            dve.wait_ge(cum_ps, 1)
            V.tensor_copy(acum[:, :], bank[5][:, 0:32]).then_inc(cum_made, 1)
            V.tensor_copy(dtot[:, :], bank[5][:, 32:64]).then_inc(cum_made, 1)
            dve.wait_ge(cum_made, 2)
            V.tensor_tensor(dend[:, :], dtot[:, :], acum[:, :], ALU.subtract).then_inc(cum_made, 1)
            V.tensor_scalar(nacum[:, :], acum[:, :], -1.0, None, ALU.mult).then_inc(cum_made, 1)

            def softmax_in(a):
                n, j = a // 4, a % 4
                lo = P if n == 0 else 0
                s3 = psum[:, 4:6, 0:2 * P]
                if a >= 2:
                    dve.wait_ge(exp_made, 3 * (a - 1))
                dve.wait_ge(sc_ps, a + 1)
                V.scalar_tensor_tensor(scores[a % 2][:, :, lo:], s3[:, :, lo:], HD ** -0.5,
                                       bias[:, j::4, lo:], ALU.mult, ALU.add).then_inc(sc_read, 1)
                dve.wait_ge(sc_read, a + 1)
                sl = slice(2 * a, 2 * a + 2)
                step(V.tensor_reduce(smax[:, sl], scores[a % 2][:, :, lo:], AX.X, ALU.max))
                step(V.tensor_tensor(smax[:, sl], smax[:, sl], v["sinks"][:, j::4], ALU.max))
                step(V.tensor_tensor(sinkd[:, sl], v["sinks"][:, j::4], smax[:, sl], ALU.subtract))
                V.tensor_scalar(nmax[:, sl], smax[:, sl], -1.0, None, ALU.mult).then_inc(nmax_made, 1)

            def softmax_out(a):
                n, j = a // 4, a % 4
                sl = slice(2 * a, 2 * a + 2)
                dve.wait_ge(exp_made, 3 * a + 3)
                step(V.tensor_tensor(rden[:, sl], psums[:, sl], esink[:, sl], ALU.add))
                step(V.reciprocal(rden[:, sl], rden[:, sl]))
                dve.wait_ge(o_ps, a + 1)
                dst = mix[:, n, D_SSD:D].rearrange("p (i j d) -> p i j d", i=2, j=4)[:, :, j, :]
                V.tensor_tensor(dst, bank[7][:, 0:P].rearrange("p (i d) -> p i d", i=2),
                                rden[:, sl].rearrange("p (i o) -> p i o", o=1)
                                .to_broadcast([P, 2, HD]), ALU.mult).then_inc(o_read, 1)

            h3 = lambda a: a.rearrange("p (h d) -> p h d", h=HEADS)
            per_head = lambda a: a.rearrange("p (h o) -> p h o", o=1).to_broadcast([P, HEADS, HD])

            def scan(c, q):
                if q in (1, 2):
                    g = q - 1
                    dve.wait_ge(decay_made, 8 * c + 4 * g + 4)
                    dve.wait_ge(tok_made, 2 * c + 2)
                    if c:
                        dve.wait_ge(y_ps, c)
                    cb = bank[1][:, 256 + P * g:256 + P * g + P].rearrange("p (o l) -> p o l", o=1)
                    V.tensor_tensor(m_t[g][:, :, :], decay[g][:, :, :], cb.to_broadcast([P, 4, P]),
                                    ALU.mult).then_inc(m_made, 1)
                elif q == 3:
                    dve.wait_ge(y_ps, c + 1)
                    dve.wait_ge(xs_made, 3 * c + 3)
                    if c == 0:
                        step(V.tensor_tensor(y_tmp[:, :], bank[3][:, :], xskip[:, :], ALU.add))
                    else:
                        step(V.tensor_tensor(h3(y_tmp[:, :]), h3(bank[2][:, :]),
                                             per_head(eacum[:, 8 * c:8 * c + 8]), ALU.mult))
                        step(V.tensor_tensor(y_tmp[:, :], y_tmp[:, :], bank[3][:, :], ALU.add))
                        step(V.tensor_tensor(y_tmp[:, :], y_tmp[:, :], xskip[:, :], ALU.add))
                    V.tensor_tensor(mix[:, c, 0:D_SSD], y_tmp[:, :], zs[:, c, :], ALU.mult
                                    ).then_inc(y_read, 1)
                    if c == 0:
                        V.tensor_copy(state[:, :], bank[0][:, :]).then_inc(state_made, 1)
                    elif c < TT - 1:
                        step(V.tensor_tensor(h3(state[:, :]), h3(state[:, :]),
                                             per_head(dtot[:, 8 * c:8 * c + 8]), ALU.mult))
                        V.tensor_tensor(state[:, :], state[:, :], bank[0][:, :], ALU.add
                                        ).then_inc(state_made, 1)

            def norm(c):
                dve.wait_ge(ssq_made, 2 * c + 2)
                V.tensor_scalar(rms[:, 2 * c:2 * c + 2], ssq[:, 2 * c:2 * c + 2], 1.0 / 512, EPS,
                                ALU.mult, ALU.add).then_inc(mean_made, 1)

            dve.wait_ge(bias_loaded, 16)
            dve.wait_ge(cum_exp, 3)
            softmax_in(0)
            softmax_in(1)
            for a in range(16):
                c, q = a // 4, a % 4
                if a + 2 < 16:
                    softmax_in(a + 2)
                scan(c, q)
                softmax_out(a)
                if q == 1 and c:
                    norm(c - 1)
            norm(TT - 1)

            for k in range(DK):
                dve.wait_ge(mix_hi_done, k + 1)
                V.scalar_tensor_tensor(mix_lo[:, k, :], bank[k][:, :], v["mix_g"][:, k:k + 1],
                                       f(mix_hi[:, k, :]), ALU.mult, ALU.subtract
                                       ).then_inc(mix_lo_done, 1)
                if k == 0:
                    low(N_IN)
            dve.wait_ge(h_loaded, 16)
            for i in range(N_OUT):
                if i + 1 < N_OUT:
                    low(N_IN + i + 1)
                dve.wait_ge(chunk_used, N_IN + i + 1)
                for half in range(2):
                    dst = h[:, 2 * half:2 * half + 2, 256 * i:256 * i + 256]
                    V.tensor_tensor(dst, dst, bank[2 * i + half][:, :].rearrange("p (t c) -> p t c", t=2),
                                    ALU.add).then_inc(h_made, 1)
            router_dve(dve, step)
            moe_dve(dve)

        @block.tensor
        def _(pe):
            MM = nc.tensor.matmul

            def three(dst, xh, xl, wh, wl, first, last):
                MM(dst, xh, wh, start=first, stop=False)
                MM(dst, xl, wh, start=False, stop=False)
                return MM(dst, xh, wl, start=False, stop=last)

            for c in range(N_IN):
                wh, wl = w_hi[c % SPLITS], w_lo[c % SPLITS]
                w3h = wh[:, :].rearrange("p (k c) -> p k c", k=DK)
                w3l = wl[:, :].rearrange("p (k c) -> p k c", k=DK)
                if c == 3:
                    pe.wait_ge(proj_evac, 2)
                elif c in (4, 5, 6):
                    pe.wait_ge(proj_evac, 2 * (c - 2))
                elif c >= 7:
                    pe.wait_ge(z_made, 4 * (c - 6))
                pe.wait_ge(lo_done, c + 1)
                b = 2 * (c % 3)

                def channels(dst, cols):
                    for k in range(DK):
                        if c == 0 and cols.start == 0:
                            pe.wait_ge(xg_lo_done, k + 1)
                        i = MM(dst, w3h[:, k, cols], xg_hi[:, k, :], start=(k == 0), stop=False)
                        i = MM(dst, w3l[:, k, cols], xg_hi[:, k, :], start=False, stop=False)
                        i = MM(dst, w3h[:, k, cols], xg_lo[:, k, :], start=False, stop=(k == DK - 1))
                    return i

                def tokens(dst, t, wh3, wl3):
                    ts = slice(P * t, P * t + P)
                    for k in range(DK):
                        i = three(dst, xg_hi[:, k, ts], xg_lo[:, k, ts], wh3[:, k, :], wl3[:, k, :],
                                  k == 0, k == DK - 1)
                    return i

                if N_XBC <= c < N_XBC + N_Z:
                    for t in range(TT):
                        ins = tokens(bank[b + t // 2][:, 256 * (t % 2):256 * (t % 2) + 256], t, w3h, w3l)
                elif c == N_XBC + N_Z:
                    channels(bank[b][:, :], slice(0, P))
                    for t in range(TT):
                        ins = tokens(bank[b + 1][:, P * t:P * t + P], t, w3h[:, :, P:2 * P],
                                     w3l[:, :, P:2 * P])
                else:
                    channels(bank[b][:, :], slice(0, P))
                    ins = channels(bank[b + 1][:, :], slice(P, 2 * P))
                ins.then_inc(chunk_used, 1)
                if c == 0:
                    pe.wait_ge(const_loaded, 80)
                    MM(bank[7][0:HEADS, 0:FW], rel[:, :], band[:, 0:FW], start=True, stop=True
                       ).then_inc(band_ps, 1)
                    pe.wait_ge(sq_done, N_X)
                    for k in range(DK):
                        ins = MM(bank[6][:, :], const["ones"], sq[:, k, :], start=(k == 0),
                                 stop=(k == DK - 1))
                    ins.then_inc(ss_ps, 1)
                if c == 1:
                    pe.wait_ge(rstd_made, 1)
                    pe.wait_ge(band_made, 1)
                    for t in range(TT):
                        ins = nc.tensor.transpose(bank[7][:, P * t:P * t + P],
                                                  rstd_row[:, P * t:P * t + P], ident)
                    ins.then_inc(rstd_t_ps, 1)
                if c == 3:
                    pe.wait_ge(rstd_tok_made, 1)
                    pe.wait_ge(wdt_lo_done, 1)
                    for k in range(DK):
                        MM(bank[7][0:HEADS, :], wdt_hi[:, k, :], xg_hi[:, k, :], start=(k == 0),
                           stop=False)
                        MM(bank[7][0:HEADS, :], wdt_lo[:, k, :], xg_hi[:, k, :], start=False, stop=False)
                        ins = MM(bank[7][0:HEADS, :], wdt_hi[:, k, :], xg_lo[:, k, :], start=False,
                                 stop=(k == DK - 1))
                    ins.then_inc(dt_ps, 1)
                if c == 5:
                    pe.wait_ge(dt_row_made, 1)
                    for t in range(TT):
                        ins = nc.tensor.transpose(bank[7][:, HEADS * t:HEADS * t + HEADS],
                                                  dt_row[:, P * t:P * t + P], ident[0:HEADS, 0:HEADS])
                    ins.then_inc(dt_t_ps, 1)

            pe.wait_ge(scan_consts_loaded, 32)
            pe.wait_ge(adt_made, 1)
            pe.wait_ge(proj_evac, 13)
            pe.wait_ge(v_made, 4)
            MM(bank[5][:, 0:32], incl[:, :], adt[:, :], start=True, stop=True)
            MM(bank[5][:, 32:64], const["ones"], adt[:, :], start=True, stop=True).then_inc(cum_ps, 1)
            pe.wait_ge(cum_made, 4)

            def attn_scores(a):
                n, j = a // 4, a % 4
                lo = P if n == 0 else 0
                if a:
                    pe.wait_ge(sc_read, a)
                for i in range(2):
                    ps = slice(HD * i, HD * i + HD)
                    ins = MM(bank[4 + i][:, lo:256], q_t[ps, j, P * n:P * n + P],
                             k_t[ps, P * n + lo:P * n + 256], start=True, stop=True)
                ins.then_inc(sc_ps, 1)

            def attn_turn(a):
                n = a // 4
                blocks = (1,) if n == 0 else (0, 1)
                pe.wait_ge(exp_made, 3 * a + 2)
                if a:
                    pe.wait_ge(pt_made, a)
                for i in range(2):
                    for kb in blocks:
                        w = 2 * i + kb if n else 2 + i
                        ins = nc.tensor.transpose(bank[6][:, P * w:P * w + P],
                                                  probs[a % 2][:, i, P * kb:P * kb + P], ident)
                ins.then_inc(pt_ps, 1)

            def attn_values(a):
                n = a // 4
                blocks = (1,) if n == 0 else (0, 1)
                pe.wait_ge(pt_made, a + 1)
                if a:
                    pe.wait_ge(o_read, a)
                for i in range(2):
                    for kb in blocks:
                        w = 2 * i + kb if n else 2 + i
                        ins = MM(bank[7][:, HD * i:HD * i + HD], probs_t[a % 2][:, w, :],
                                 v_tok[:, n + kb, HD * i:HD * i + HD], start=(kb == blocks[0]),
                                 stop=(kb == 1))
                ins.then_inc(o_ps, 1)

            def scan(c, q):
                cs = slice(P * c, P * c + P)
                if q == 0:
                    if c:
                        pe.wait_ge(state_made, c)
                        pe.wait_ge(m_made, 2 * c)
                    for i in range(4):
                        nc.tensor.transpose(bank[0][:, P * i:P * i + P], xbc[:, i, cs], ident)
                    for g in range(2):
                        nc.tensor.transpose(bank[1][:, P * g:P * g + P], xbc[:, 4 + g, cs], ident)
                    for g in range(2):
                        ins = MM(bank[1][:, 256 + P * g:256 + P * g + P], xbc[:, 4 + g, cs],
                                 xbc[:, 6 + g, cs], start=True, stop=True)
                    ins.then_inc(tok_ps, 1)
                if q in (1, 2):
                    g = q - 1
                    if 2 * c + g:
                        pe.wait_ge(decay_made, 4 * (2 * c + g))
                    if c:
                        pe.wait_ge(y_read, c)
                    MM(bank[2][:, :].rearrange("p (r l) -> p r l", r=4), ident,
                       negmask[:, :].rearrange("p (o l) -> p o l", o=1).to_broadcast([P, 4, P]),
                       start=True, stop=False)
                    for r in range(4):
                        jj = 8 * c + 4 * g + r
                        ins = MM(bank[2][:, P * r:P * r + P], adt[:, jj:jj + 1].to_broadcast([P, P]),
                                 incl[:, :], start=False, stop=(r == 3))
                    ins.then_inc(bc_ps, 1)
                if q in (2, 3):
                    g = q - 2
                    pe.wait_ge(m_made, 2 * c + g + 1)
                    pe.wait_ge(xs_made, 3 * c + 3)
                    if c:
                        pe.wait_ge(y_read, c)
                    for r in range(4):
                        hs = slice(HD * (4 * g + r), HD * (4 * g + r) + HD)
                        ins = MM(bank[3][:, hs], m_t[g][:, r, :], xdt[:, hs], start=True, stop=True)
                if q == 3:
                    if c:
                        pe.wait_ge(decay_made, 8 * c + 8)
                        for g in range(2):
                            ins = MM(bank[2][:, 256 * g:256 * g + 256], xbc[:, 6 + g, cs],
                                     state[:, 256 * g:256 * g + 256], start=True, stop=True)
                    if c < TT - 1:
                        for g in range(2):
                            ins = MM(bank[0][:, 256 * g:256 * g + 256], b_toks[c % 2][:, g, :],
                                     xdd[:, 256 * g:256 * g + 256], start=True, stop=True)
                    ins.then_inc(y_ps, 1)

            attn_scores(0)
            attn_scores(1)
            for a in range(16):
                attn_turn(a)
                if a + 2 < 16:
                    attn_scores(a + 2)
                scan(a // 4, a % 4)
                attn_values(a)

            pe.wait_ge(y_read, TT)
            pe.wait_ge(o_read, 16)
            pe.wait_ge(normed, 2 * TT - 2)
            for t in range(TT - 1):
                for k in range(DK):
                    nc.tensor.transpose(bank[k][:, P * t:P * t + P], mix[:, t, P * k:P * k + P], ident)
            pe.wait_ge(normed, 2 * TT)
            for k in range(DK):
                nc.tensor.transpose(bank[k][:, T - P:T], mix[:, TT - 1, P * k:P * k + P], ident
                                    ).then_inc(mix_ps, 1)
            for i in range(N_OUT):
                c = N_IN + i
                pe.wait_ge(lo_done, c + 1)
                w3h = w_hi[c % SPLITS][:, :].rearrange("p (k c) -> p k c", k=DK)
                w3l = w_lo[c % SPLITS][:, :].rearrange("p (k c) -> p k c", k=DK)
                for t in range(TT):
                    ts = slice(P * t, P * t + P)
                    for k in range(DK):
                        if i == 0 and t == 0:
                            pe.wait_ge(mix_lo_done, max(k + 1, 2))
                        ins = three(bank[2 * i + t // 2][:, 256 * (t % 2):256 * (t % 2) + 256],
                                    mix_hi[:, k, ts], mix_lo[:, k, ts], w3h[:, k, :], w3l[:, k, :],
                                    k == 0, k == DK - 1)
                ins.then_inc(chunk_used, 1)
            router_pe(pe, three)
            moe_pe(pe)


def kernel(x, norm_mix_g, w_in, conv_w, conv_b, dt_bias, a_log, d_skip, ssd_norm_g, attn_sinks,
           rel_bias, attn_norm_g, w_out, norm_ffn_g, w_router, b_router, w1, b1, w2, b2,
           norm_final_g):
    import concourse.bacc as bacc
    from concourse.bass_utils import run_bass_kernel_spmd

    x, w_in, w_out, w1, w2 = (np.asarray(a) for a in (x, w_in, w_out, w1, w2))
    f = np.float32
    o1, o2 = D_SSD, D_SSD + 2 * D_SSD
    o3 = o2 + HEADS
    o4 = o3 + D_SSD
    wi = w_in[0]
    q = wi[:, o3:o4].reshape(D, 2, 4, HD).transpose(0, 2, 1, 3).reshape(D, D_SSD)
    cols = np.concatenate([wi[:, o1:o2], wi[:, :o1], wi[:, o4:], q], 1)
    stream = np.empty((N_PRO + E * PER_EXPERT, P, CHUNK), f)
    stream[0:2] = x[0].T.reshape(2, 4, P, T).transpose(0, 2, 1, 3).reshape(2, P, CHUNK)
    stream[2:2 + N_IN] = cols.reshape(DK, P, N_IN, 256).transpose(2, 1, 0, 3).reshape(N_IN, P, CHUNK)
    stream[C_OUT:N_PRO] = w_out[0].reshape(DK, P, N_OUT, 256).transpose(2, 1, 0, 3).reshape(
        N_OUT, P, CHUNK)
    w1v = w1[0].reshape(E, 4, 2, P, 2, 2, 512).transpose(0, 5, 1, 3, 2, 4, 6)
    w2v = w2[0].reshape(E, 4, 2, P, D).transpose(0, 1, 3, 2, 4)
    moe = stream[N_PRO:]
    moe[0:4] = w1v[0, 0].reshape(4, P, CHUNK)
    for e in range(E):
        last = e == E - 1
        a = moe[4 + PER_EXPERT * e:]
        a[0:4] = w1v[e, 1].reshape(4, P, CHUNK)
        a[4:6] = w2v[e, 0:2].reshape(2, P, CHUNK)
        if not last:
            a[6:10] = w1v[e + 1, 0].reshape(4, P, CHUNK)
        k = 6 if last else 10
        a[k:k + 2] = w2v[e, 2:4].reshape(2, P, CHUNK)
    w_dt = np.ascontiguousarray(wi[:, o2:o3].reshape(DK, P, HEADS).transpose(1, 0, 2))

    def by_partition(a, n):
        return np.asarray(a).reshape(n, P).T

    def rows(a):
        return np.broadcast_to(np.asarray(a).reshape(1, -1), (P, np.asarray(a).size))

    parts = {
        "norm_mix_g": by_partition(norm_mix_g, DK),
        "conv_w": np.asarray(conv_w)[0].reshape(4, 8, P).transpose(2, 1, 0).reshape(P, 32),
        "conv_b": by_partition(conv_b, 8),
        "mix_g": np.concatenate([by_partition(ssd_norm_g, 4), by_partition(attn_norm_g, 4)], 1),
        "dt_bias": rows(dt_bias), "a_log": rows(a_log), "d_skip": rows(d_skip),
        "sinks": rows(attn_sinks), "b_router": rows(b_router),
    }
    vectors = np.ascontiguousarray(np.concatenate([parts[n] for n, _ in VECTORS], 1))
    packed, where = shape_constants()
    order = MAIN_CONSTS + MIXER_CONSTS + ("band", "neg")
    consts = np.ascontiguousarray(np.concatenate(
        [packed[:, where[n][0]:where[n][0] + where[n][1]] for n in order], 1))
    arrays = {
        "stream": stream, "x": np.asarray(x)[0], "w_dt": w_dt, "vectors": vectors, "consts": consts,
        "rel_bias": rel_bias, "norm_ffn_g": np.asarray(norm_ffn_g)[0], "norm_final_g": norm_final_g,
        "w_router": np.asarray(w_router)[0], "b1": np.asarray(b1)[0], "b2": np.asarray(b2)[0],
    }
    arrays = {k: np.ascontiguousarray(a) for k, a in arrays.items()}
    nc = bacc.Bacc("TRN2", target_bir_lowering=False, num_devices=1)
    args = [nc.dram_tensor(k, a.shape, mybir.dt.from_np(a.dtype), kind="ExternalInput").ap()
            for k, a in arrays.items()]
    y = nc.dram_tensor("y", (T, D), F32, kind="ExternalOutput").ap()
    build(nc, *args, y)
    r = run_bass_kernel_spmd(nc, [arrays], core_ids=[0])
    return r.results[0]["y"].reshape(1, T, D)
```

```python
import math
from contextlib import ExitStack

import numpy as np

import concourse.bass as bass
from concourse import mybir

F32 = mybir.dt.float32
F32R = mybir.dt.float32r
U32 = mybir.dt.uint32
ALU = mybir.AluOpType
ACT = mybir.ActivationFunctionType
AX = mybir.AxisListType

P = 128
T = 512
TT = T // P
D = 1024
DK = D // P
D_SSD = 512
HEADS = 8
HD = 64
STATE = 128
E = 32
TOPK = 4
EPS = 1e-5
NEG = -1e30
BUCKETS = 32
WINDOW = 128
CHUNK = 2048
FW = 3 * P - 1

N_X = 2
N_XBC, N_Z, N_KV, N_Q = 4, 2, 1, 2
N_IN = N_XBC + N_Z + N_KV + N_Q
N_OUT = 4
N_PRO = N_X + N_IN + N_OUT
C_IN = N_X
C_OUT = N_X + N_IN
PRO_SLOTS = 9
PER_EXPERT = 12
SLOTS = 12
EXPERT_SLOT = [(6 + m) % PRO_SLOTS for m in range(PRO_SLOTS)] + [9, 10, 11]
SPLITS = 3


def t5_bucket(dist):
    max_exact = BUCKETS // 2
    d = np.maximum(dist, 1).astype(np.float32)
    large = max_exact + (np.log(d / np.float32(max_exact)) / np.float32(math.log(128 / max_exact))
                         * np.float32(BUCKETS - max_exact)).astype(np.int32)
    return np.where(dist < max_exact, dist, np.minimum(large, BUCKETS - 1))


def shape_constants():
    i = np.arange(P)
    f = np.float32
    band = np.zeros((BUCKETS + 1, FW), f)
    for j in range(FW):
        dist = 2 * P - 1 - j
        if 0 <= dist < WINDOW:
            band[t5_bucket(np.array(dist)), j] = 1
        else:
            band[BUCKETS, j] = 1
    tokens = (i[:, None] + P * np.arange(TT)[None, :]).astype(f)
    parts = {
        "ident": np.eye(P, dtype=f),
        "incl": (i[:, None] <= i[None, :]).astype(f),
        "strict": (i[:, None] < i[None, :]).astype(f),
        "ones": np.ones((P, P), f),
        "slots": np.broadcast_to(i.astype(f), (P, P)),
        "negmask": np.where(i[:, None] > i[None, :], f(NEG), f(0)),
        "band": np.concatenate([band, np.zeros((P - BUCKETS - 1, FW), f)]),
        "neg": np.full((P, HEADS), NEG, f),
        "experts": np.broadcast_to(np.arange(E, dtype=f), (P, E)),
        "tokens": tokens,
        "trash": (T + i[:, None]).astype(f),
        "rows2e": (i[:, None] % E == np.arange(E)[None, :]).astype(f) * (i[:, None] < 2 * E),
    }
    at, where = 0, {}
    for name, a in parts.items():
        where[name] = (at, a.shape[1])
        at += a.shape[1]
    return np.ascontiguousarray(np.concatenate(list(parts.values()), 1).astype(f)), where


MAIN_CONSTS = ("ident", "strict", "ones", "slots", "experts", "tokens", "trash", "rows2e")
MIXER_CONSTS = ("incl", "negmask")
VECTORS = (("norm_mix_g", DK), ("conv_w", 32), ("conv_b", 8), ("mix_g", DK), ("dt_bias", HEADS),
           ("a_log", HEADS), ("d_skip", HEADS), ("sinks", HEADS), ("b_router", E),
           ("norm_ffn_g", DK))


def build(nc, stream, x, w_dt, vectors, consts, rel_bias, norm_ffn_g, norm_final_g, w_router,
          b1, b2, out):
    _, where = shape_constants()

    band_dram = nc.dram_tensor("band_dram", [P, HEADS * FW], F32)
    u_dram = nc.dram_tensor("u_dram", [T, D], F32)
    acc_dram = nc.dram_tensor("acc_dram", [T + P, D], F32)

    base = (nc.sbuf_base + 63) // 64 * 64

    def at(name, shape, dtype, offset):
        return nc.alloc_sbuf_tensor_at(name, shape, dtype, offset=base + offset)

    RING, HI, LO = 0, 73728, 98304
    SMALL = 122880
    A = SMALL + 5632
    F = A + 24576
    ring = [at(f"ring{s}", [P, CHUNK], F32, RING + 8192 * s) for s in range(PRO_SLOTS)] + \
           [at(f"ring{s}", [P, CHUNK], F32, A + 8192 * (s - PRO_SLOTS)) for s in range(PRO_SLOTS, SLOTS)]
    w_hi = [at(f"w_hi{s}", [P, CHUNK], F32R, HI + 8192 * s) for s in range(SPLITS)]
    w_lo = [at(f"w_lo{s}", [P, CHUNK], F32R, LO + 8192 * s) for s in range(SPLITS)]

    off = SMALL
    main_w = sum(where[n][1] for n in MAIN_CONSTS)
    vec_w = sum(w for _, w in VECTORS)
    main = at("main", [P, main_w], F32, off); off += (4 * main_w + 31) // 32 * 32
    vec = at("vec", [P, vec_w], F32, off); off += (4 * vec_w + 31) // 32 * 32
    slot_rhs = at("slot_rhs", [P, TT, E, 4], F32, off); off += 16 * TT * E
    pos = at("pos", [P, TT, E], F32, off); off += 4 * TT * E
    smalls_end = off
    assert off <= A, (off, A)
    const = {}
    col = 0
    for n in MAIN_CONSTS:
        const[n] = main[:, col:col + where[n][1]]
        col += where[n][1]
    v = {}
    col = 0
    for n, w in VECTORS:
        v[n] = vec[:, col:col + w]
        col += w
    ident = const["ident"]

    xg_hi = at("xg_hi", [P, DK, T], F32R, A)
    xg_lo = at("xg_lo", [P, DK, T], F32R, A + 16384)
    B = A + 32768
    xbc = at("xbc", [P, 8, T], F32, B)
    zs = at("zs", [P, TT, D_SSD], F32, B + 16384)
    q_t = at("q_t", [P, 4, T], F32, B + 24576)
    sq = at("sq", [P, DK, T], F32, B + 16384)
    k_t = at("k_t", [P, P + T], F32, B + 32768)
    v_tok = at("v_tok", [P, TT + 1, P], F32, B + 35328)
    conv_in = at("conv_in", [P, 2, T + 4], F32, B + 37888)
    conv_acc = at("conv_acc", [P, 2, T], F32, B + 42016)
    rstd_row = at("rstd_row", [P, T], F32, B + 46112)
    off = B + 48160
    band = at("band", [BUCKETS + 1, FW + 1], F32, off); off += 4 * (FW + 1)
    wdt = at("wdt", [P, DK, HEADS], F32, off); off += 256
    wdt_hi = at("wdt_hi", [P, DK, HEADS], F32R, off); off += 256
    wdt_lo = at("wdt_lo", [P, DK, HEADS], F32R, off); off += 256
    rstd_tok = at("rstd_tok", [P, TT], F32, off); off += 32
    assert off - A <= 83456, off - A
    dt_raw, dt_e, dt_u, dt_d, dt_l, dt, adt, acum, nacum, eacum, dend, dtot = (
        at(n, [P, 32], F32, B + 48160 + 128 * i) for i, n in enumerate((
            "dt_raw", "dt_e", "dt_u", "dt_d", "dt_l", "dt", "adt", "acum", "nacum", "eacum",
            "dend", "dtot")))
    incl = at("incl", [P, P], F32, B + 48160 + 1536)
    a_neg = at("a_neg", [P, HEADS], F32, B + 48160 + 1536 + 512)
    band_rows = at("band_rows", [HEADS, FW + 1], F32, B)
    dt_row = at("dt_row", [HEADS, T], F32, B + 24576)
    rel = at("rel", [BUCKETS + 1, HEADS], F32, B + 46112)

    S = HI
    x_tok = at("x_tok", [P, D_SSD], F32, S)
    x_tok2 = at("x_tok2", [P, D_SSD], F32, S + 2048)
    b_tok = at("b_tok", [P, 2, STATE], F32, S + 4096)
    b_tok2 = at("b_tok2", [P, 2, STATE], F32, S + 5120)
    x_toks, b_toks = [x_tok, x_tok2], [b_tok, b_tok2]
    xdt = at("xdt", [P, D_SSD], F32, S + 6144)
    xdd = at("xdd", [P, D_SSD], F32, S + 8192)
    xskip = at("xskip", [P, D_SSD], F32, S + 10240)
    decay = [at(f"decay{g}", [P, 4, P], F32, S + 12288 + 2048 * g) for g in range(2)]
    m_t = [at(f"m_t{g}", [P, 4, P], F32, S + 16384 + 2048 * g) for g in range(2)]
    state = at("state", [P, D_SSD], F32, S + 20480)
    y_tmp = at("y_tmp", [P, D_SSD], F32, S + 22528)
    scores = [at(f"scores{i}", [P, 2, 2 * P], F32, S + 24576 + 2048 * i) for i in range(2)]
    probs = [at(f"probs{i}", [P, 2, 2 * P], F32, S + 28672 + 2048 * i) for i in range(2)]
    probs_t = [at(f"probs_t{i}", [P, 4, P], F32, S + 32768 + 2048 * i) for i in range(2)]
    negmask = at("negmask", [P, P], F32, S + 37376)
    negmask_r = at("negmask_r", [P, P], F32R, S + 37888)
    ident_r = at("ident_r", [P, P], F32R, S + 38400)
    off = S + 38912

    def small(name, cols, dtype=F32):
        nonlocal off
        t = at(name, [P, cols], dtype, off)
        off += (4 * cols + 31) // 32 * 32
        return t

    smax = small("smax", 32)
    nmax = small("nmax", 32)
    sinkd = small("sinkd", 32)
    psums = small("psums", 32)
    esink = small("esink", 32)
    rden = small("rden", 32)
    ssq = small("ssq", 8)
    rms = small("rms", 8)
    sq_junk = small("sq_junk", D_SSD)
    assert off <= SMALL, off
    bias = at("bias", [P, HEADS, 2 * P], F32, B + 37888)
    mix = at("mix", [P, TT, D], F32, A + 16384)
    mix_hi = at("mix_hi", [P, DK, T], F32R, B)
    mix_lo = at("mix_lo", [P, DK, T], F32R, B + 16384)
    h = at("h", [P, TT, D], F32, A)
    u2 = [at(f"u2_{t}", [P, D], F32, (A + 16384 if t < 2 else B) + 4096 * t) for t in range(TT)]
    b2_hl = at("b2_hl", [3 * E, D], F32R, B + 16384)
    gates_hl = at("gates_hl", [3 * E, T], F32R, B + 20480)
    pick = at("pick", [P, TT, TOPK, E], F32, B + 22528)
    h_t = [at(f"h_t{i}", [P, DK, P], F32, A + 24576 + 4096 * i) for i in range(2)]
    R = B + 32768
    ffn_g = at("ffn_g", [P, D], F32, R)
    wr = at("wr", [P, DK, E], F32, R + 4096)
    off = R + 5120
    logits = small("logits", TT * E)
    top = small("top", TT * 8)
    top_idx = small("top_idx", TT * 8, U32)
    top_f = small("top_f", TT * 8)
    gexp = small("gexp", TT * 4)
    gsum = small("gsum", TT)
    gate = small("gate", TT * 4)
    mask = small("mask", TT * E)
    gates = small("gates", TT * 3 * E)
    ssq2 = small("ssq2", 2 * TT)
    rms2 = small("rms2", TT)
    b2_sb = at("b2_sb", [3 * E, D], F32, off); off += 4096
    assert off <= R + 14464, off - R
    y_sb = [at(f"y_sb{i}", [P, D], F32, F + 4096 * i) for i in range(2)]
    b1_hl = at("b1_hl", [2 * E, 2 * D], F32R, B)
    xe = [at(f"xe{i}", [P, D], F32, B + 8192 + 4096 * i) for i in range(2)]
    xe_hi = [at(f"xe_hi{i}", [P, DK, P], F32R, B + 16384 + 4096 * i) for i in range(2)]
    xe_lo = [at(f"xe_lo{i}", [P, DK, P], F32R, B + 24576 + 4096 * i) for i in range(2)]
    b1_raw = at("b1_raw", [2 * E, 2 * D], F32, B + 24576)
    glu = at("glu", [P, T], F32, R)
    lin = at("lin", [P, T], F32, R + 2048)
    sig = at("sig", [P, T], F32, R + 4096)
    hid_hi = [at(f"hid_hi{i}", [P, 4, P], F32R, R + 6144 + 2048 * i) for i in range(2)]
    hid_lo = [at(f"hid_lo{i}", [P, 4, P], F32R, R + 10240 + 2048 * i) for i in range(2)]
    onehot = at("onehot", [P, TT, P], F32, R + 14464)
    sel = [at(f"sel{i}", [2 * E, P], F32R, R + 16512 + 512 * i) for i in range(2)]
    off = R + 17536
    slot_gate = small("slot_gate", E)
    slot_token = small("slot_token", E, U32)
    slot_row = small("slot_row", E, U32)
    assert off <= A + 83456, off - A

    off = smalls_end
    power = small("power", 4)
    n_max = small("n_max", 1)
    n_max_u = small("n_max_u", 1, U32)
    valid = small("valid", 1)
    assert off <= A, off
    off = A + 83456
    fin_ssq_t = small("fin_ssq_t", TT)
    fin_rms_t = small("fin_rms_t", TT)
    assert base + off <= nc.sbuf_usable_end
    fin = [at(f"fin{t}", [P, D], F32, RING + 4096 * t) for t in range(TT)]
    fin_g = at("fin_g", [P, D], F32, RING + 16384)
    fin_junk = at("fin_junk", [P, D], F32, RING + 20480)

    psum = nc.alloc_psum_tensor("psum", [P, 8, 512], F32)
    bank = [psum[:, i, :] for i in range(8)]

    with ExitStack() as ctx:
        def sem(name):
            return ctx.enter_context(nc.semaphore(name))

        const_loaded = sem("const_loaded")
        w_loaded = [sem(f"w_loaded{s}") for s in range(SLOTS)]
        band_stored, bias_loaded, scan_consts_loaded, h_loaded = map(
            sem, ("band_stored", "bias_loaded", "scan_consts_loaded", "h_loaded"))
        router_loaded, b1_loaded = map(sem, ("router_loaded", "b1_loaded"))
        acc_stored = [sem(f"acc_stored_{i}") for i in range(2)]
        u_stored = [sem(f"u_stored_{i}") for i in range(2)]
        xg_hi_done, xg_lo_done, sq_done, hi_done, lo_done, chunk_used = map(
            sem, ("xg_hi_done", "xg_lo_done", "sq_done", "hi_done", "lo_done", "chunk_used"))
        vec_loaded, band_ps, band_made, pads_made, ss_ps, rstd_made, rstd_t_ps, rstd_tok_made = map(
            sem, ("vec_loaded", "band_ps", "band_made", "pads_made", "ss_ps", "rstd_made",
                  "rstd_t_ps", "rstd_tok_made"))
        dt_row_made, dt_t_ps, mask_rounded = map(sem, ("dt_row_made", "dt_t_ps", "mask_rounded"))
        wr_scaled, u_scaled, u_late = map(sem, ("wr_scaled", "u_scaled", "u_late"))
        sq_summed, trash_stored, incl_loaded = map(sem, ("sq_summed", "trash_stored", "incl_loaded"))
        b2_hi_done, b2_lo_done, gates_made, gates_hi_made = map(
            sem, ("b2_hi_done", "b2_lo_done", "gates_made", "gates_hi_made"))
        proj_evac, z_made, v_made, conv_done, silu_done, wdt_hi_done, wdt_lo_done, dt_ps = map(
            sem, ("proj_evac", "z_made", "v_made", "conv_done", "silu_done", "wdt_hi_done",
                  "wdt_lo_done", "dt_ps"))
        dve_step = sem("dve_step")
        dt_arg, dt_exp, dt_one, dt_log, a_exp, adt_made, cum_ps, cum_made, cum_exp = map(
            sem, ("dt_arg", "dt_exp", "dt_one", "dt_log", "a_exp", "adt_made", "cum_ps",
                  "cum_made", "cum_exp"))
        tok_ps, tok_made, xs_made, bc_ps, decay_made, m_made, y_ps, y_read, state_made = map(
            sem, ("tok_ps", "tok_made", "xs_made", "bc_ps", "decay_made", "m_made", "y_ps",
                  "y_read", "state_made"))
        sc_ps, sc_read, nmax_made, exp_made, pt_ps, pt_made, o_ps, o_read = map(
            sem, ("sc_ps", "sc_read", "nmax_made", "exp_made", "pt_ps", "pt_made", "o_ps", "o_read"))
        ssq_made, mean_made, rms_made, normed = map(
            sem, ("ssq_made", "mean_made", "rms_made", "normed"))
        ms_made, rms_root = map(sem, ("ms_made", "rms_root"))
        mix_ps, mix_hi_done, mix_lo_done, h_made = map(
            sem, ("mix_ps", "mix_hi_done", "mix_lo_done", "h_made"))
        h_ssq, u_made, h_t_ps, h_t_made, logit_ps = map(
            sem, ("h_ssq", "u_made", "h_t_ps", "h_t_made", "logit_ps"))
        top_made, top_exp, mask_made, pos_ps, pos_made, gates_t_ps, gates_t_made = map(
            sem, ("top_made", "top_exp", "mask_made", "pos_ps", "pos_made", "gates_t_ps",
                  "gates_t_made"))
        rhs_filled, count_made, b2_ps, acc_made, b1_hi_done, b1_lo_done, h_rms = map(
            sem, ("rhs_filled", "count_made", "b2_ps", "acc_made", "b1_hi_done", "b1_lo_done", "h_rms"))
        out_stored = sem("out_stored")
        onehot_made, sel_made, slot_ps, slot_info = map(
            sem, ("onehot_made", "sel_made", "slot_ps", "slot_info"))
        xe_loaded = [sem(f"xe_loaded{i}") for i in range(2)]
        xt_ps, xt_hi_made, xt_lo_made, glu_made, lin_made, u_half, sig_made, hid_made = map(
            sem, ("xt_ps", "xt_hi_made", "xt_lo_made", "glu_made", "lin_made", "u_half", "sig_made",
                  "hid_made"))
        hid_t_ps, hid_hi_made, hid_lo_made, scattered, slot_parts = map(
            sem, ("hid_t_ps", "hid_hi_made", "hid_lo_made", "scattered", "slot_parts"))
        moe_over, acc_loaded, fin_ssq, fin_mean, fin_rms, fin_made, pos_shifted = map(
            sem, ("moe_over", "acc_loaded", "fin_ssq", "fin_mean", "fin_rms", "fin_made",
                  "pos_shifted"))
        h_mean, y_made_half = map(sem, ("h_mean", "y_made_half"))
        fin_loaded = [sem(f"fin_loaded{t}") for t in range(TT)]

        block = ctx.enter_context(nc.Block())

        def silu_tiles(c):
            return (2 * c, 2 * c + 1)

        TURN = (0, 2, 6)

        def router_act(act):
            A_ = nc.scalar.activation
            def squares(part, cols):
                for t in range(TT):
                    if t >= 2:
                        act.wait_ge(h_ssq, TT * part + t - 1)
                    A_(u2[t % 2][:, cols], h[:, t, cols], ACT.Square,
                       accum_out=ssq2[:, TT * part + t:TT * part + t + 1]).then_inc(h_ssq, 1)

            def turned(t):
                act.wait_ge(h_t_ps, t + 1)
                if t >= 2:
                    act.wait_ge(logit_ps, t - 1)
                for i in range(2):
                    A_(h_t[t % 2][:, 4 * i:4 * i + 4, :].rearrange("p k t -> p (k t)"),
                       bank[TURN[t % 3] + i], ACT.Copy).then_inc(h_t_made, 1)

            expert0_high(act, 0)
            act.wait_ge(h_made, 2 * (N_OUT - 1))
            squares(0, slice(0, 768))
            expert0_high(act, 1)
            expert0_high(act, 2)
            turned(0)
            act.wait_ge(router_loaded, 80)
            act.wait_ge(chunk_used, N_IN + N_OUT)
            A_(b2_hl[:, :], b2_sb[:, :], ACT.Copy).then_inc(b2_hi_done, 1)
            turned(1)
            act.wait_ge(h_made, 2 * N_OUT)
            squares(1, slice(768, D))
            turned(2)
            act.wait_ge(h_rms, 1)
            for t in (2, 3):
                A_(u2[t][:, :], h[:, t, :], ACT.Copy, scale=rms2[:, t:t + 1]).then_inc(u_scaled, 1)
                if t == 2:
                    turned(3)
            act.wait_ge(b1_loaded, 32)
            A_(b1_hl[:, :], b1_raw[:, :], ACT.Copy).then_inc(b1_hi_done, 1)
            act.wait_ge(top_made, 1)
            A_(gexp[:, :], gexp[:, :], ACT.Exp).then_inc(top_exp, 1)
            act.wait_ge(gates_t_ps, 1)
            A_(gates_hl[:, :], bank[6][0:3 * E, :], ACT.Copy).then_inc(gates_hi_made, 1)

        def router_dve(dve, mark, step, steps):
            V = nc.vector
            low_of(dve, EXPERT_SLOT[2], LEAD + 3, (LEAD + 2) % SPLITS)
            dve.wait_ge(b2_hi_done, 1)
            V.tensor_tensor(b2_hl[2 * E:3 * E, :], b2_sb[2 * E:3 * E, :],
                            b2_hl[2 * E:3 * E, :].bitcast(F32), ALU.subtract).then_inc(b2_lo_done, 1)
            dve.wait_ge(h_ssq, 2 * TT)
            step(V.tensor_tensor(rms2[:, :], ssq2[:, 0:TT], ssq2[:, TT:2 * TT], ALU.add))
            V.tensor_scalar(rms2[:, :], rms2[:, :], 1.0 / D, EPS, ALU.mult, ALU.add).then_inc(h_mean, 1)
            dve.wait_ge(h_rms, 1)
            for t in range(2):
                V.scalar_tensor_tensor(u2[t][:, :], h[:, t, :], rms2[:, t:t + 1], ffn_g[:, :],
                                       ALU.mult, ALU.mult).then_inc(u_made, 1)
            dve.wait_ge(logit_ps, TT)
            t3 = lambda a, w: a.rearrange("p (t e) -> p t e", t=TT)
            step(V.tensor_tensor(t3(logits[:, :], E), t3(bank[4][:, 0:TT * E], E),
                                 rms2[:, :].rearrange("p (t o) -> p t o", o=1)
                                 .to_broadcast([P, TT, E]), ALU.mult))
            step(V.tensor_tensor(t3(logits[:, :], E), t3(logits[:, :], E), v["b_router"].rearrange(
                "p (o e) -> p o e", o=1).to_broadcast([P, TT, E]), ALU.add))
            lg = lambda t: logits[:, E * t:E * t + E]
            for t in range(TT):
                mark(V.max(out=top[:, 8 * t:8 * t + 8], in_=lg(t)))
            dve.wait_ge(dve_step, steps[0])
            top3 = top[:, :].rearrange("p (t j) -> p t j", t=TT)
            g3 = lambda a: a[:, :].rearrange("p (t j) -> p t j", t=TT)
            V.tensor_tensor(g3(gexp), top3[:, :, 0:TOPK], top3[:, :, 0:1].to_broadcast([P, TT, TOPK]),
                            ALU.subtract).then_inc(top_made, 1)
            for t in range(TT):
                mark(V.max_index(out=top_idx[:, 8 * t:8 * t + 8], in_max=top[:, 8 * t:8 * t + 8],
                                 in_values=lg(t)))
            dve.wait_ge(dve_step, steps[0])
            step(V.tensor_copy(top_f[:, :], top_idx[:, :]))
            all4 = [P, TT, TOPK, E]
            step(V.tensor_tensor(
                pick[:, :, :, :],
                const["experts"].rearrange("p (a b e) -> p a b e", a=1, b=1).to_broadcast(all4),
                g3(top_f)[:, :, 0:TOPK].rearrange("p t (j o) -> p t j o", o=1).to_broadcast(all4),
                ALU.is_equal))
            V.tensor_reduce(g3(mask), pick[:, :, :, :].rearrange("p t j e -> p t e j"), AX.X, ALU.add
                            ).then_inc(mask_made, 1)
            dve.wait_ge(top_exp, 1)
            step(V.tensor_reduce(gsum[:, :], g3(gexp), AX.X, ALU.add))
            step(V.reciprocal(gsum[:, :], gsum[:, :]))
            step(V.tensor_tensor(g3(gate), g3(gexp), gsum[:, :].rearrange("p (t o) -> p t o", o=1)
                                 .to_broadcast([P, TT, TOPK]), ALU.mult))
            dve.wait_ge(mask_made, 1)
            step(V.tensor_tensor(pick[:, :, :, :], pick[:, :, :, :],
                                 g3(gate).rearrange("p t (j o) -> p t j o", o=1).to_broadcast(all4),
                                 ALU.mult))
            gates3 = gates[:, :].rearrange("p (t i e) -> p t i e", t=TT, i=3)
            step(V.tensor_reduce(gates3[:, :, 0, :], pick[:, :, :, :].rearrange("p t j e -> p t e j"),
                                 AX.X, ALU.add))
            V.tensor_copy(gates3[:, :, 1:3, :], gates3[:, :, 0:1, :].to_broadcast([P, TT, 2, E])
                          ).then_inc(gates_made, 1)
            dve.wait_ge(rhs_filled, 4)
            mark(V.tensor_copy(slot_rhs[:, :, :, 1], gates3[:, :, 0, :]))
            dve.wait_ge(pos_ps, 1)
            step(V.scalar_tensor_tensor(pos[:, :, :].rearrange("p t e -> p (t e)"),
                                        bank[5][:, 0:TT * E], 1.0, mask[:, :], ALU.add, ALU.mult))
            V.tensor_scalar(pos[:, :, :], pos[:, :, :], -1.0, None, ALU.add).then_inc(pos_made, 1)
            step(V.tensor_reduce(n_max[:, :], bank[5][:, TT * E:TT * E + E], AX.X, ALU.max))
            V.tensor_copy(n_max_u[:, :], n_max[:, :]).then_inc(count_made, 1)

        def router_pe(pe, three):
            MM = nc.tensor.matmul

            def turn(t, first=0, last=DK):
                for k in range(first, last):
                    ins = nc.tensor.transpose(bank[TURN[t % 3] + k // 4][:, P * (k % 4):P * (k % 4) + P],
                                              h[:, t, P * k:P * k + P], ident)
                if last == DK:
                    ins.then_inc(h_t_ps, 1)

            pe.wait_ge(h_made, 2 * (N_OUT - 1))
            turn(0, 0, 6)
            turn(1, 0, 6)
            pe.wait_ge(h_made, 2 * N_OUT)
            turn(0, 6)
            turn(1, 6)
            turn(2)
            pe.wait_ge(wr_scaled, 1)
            for t in range(TT):
                if t == 1:
                    pe.wait_ge(h_t_made, 2)
                    turn(3)
                pe.wait_ge(h_t_made, 2 * (t + 1))
                for k in range(DK):
                    ins = MM(bank[4][:, E * t:E * t + E], h_t[t % 2][:, k, :], wr[:, k, :],
                             start=(k == 0), stop=(k == DK - 1))
                ins.then_inc(logit_ps, 1)
            pe.wait_ge(mask_made, 1)
            n = TT * E
            MM(bank[5][:, 0:E], const["strict"], mask[:, 0:E], start=True, stop=True)
            MM(bank[5][:, E:n], const["strict"], mask[:, E:n], start=True, stop=False)
            for s in range(TT, 0, -1):
                ins = MM(bank[5][:, E * s:n + E], const["ones"], mask[:, 0:n + E - E * s], start=False,
                         stop=(s == 1))
            ins.then_inc(pos_ps, 1)
            pe.wait_ge(gates_made, 1)
            for t in range(TT):
                ins = nc.tensor.transpose(bank[6][0:3 * E, P * t:P * t + P],
                                          gates[:, 3 * E * t:3 * E * t + 3 * E], ident)
            ins.then_inc(gates_t_ps, 1)

        LEAD = N_IN + N_OUT
        IT = LEAD + 4
        PRO_USES = [(N_PRO - s + PRO_SLOTS - 1) // PRO_SLOTS for s in range(PRO_SLOTS)] + [0] * 3
        PAIRS = E // 2
        EARLY = 3
        GLU, LINEAR = (0, 2), (1, 3)
        Y0, HT, XT = 4, 6, 7

        def later(g):
            return not isinstance(g, int) or g > 0

        def chunk_slot(j):
            place = (4 + j) % PER_EXPERT
            return EXPERT_SLOT[place], PRO_USES[EXPERT_SLOT[place]] + (4 + j) // PER_EXPERT, (IT + j) % SPLITS

        def high_of(act, ringslot, loads, count, parts):
            act.wait_ge(w_loaded[ringslot], loads)
            act.wait_ge(chunk_used, count - SPLITS)
            nc.scalar.activation(w_hi[parts][:, :], ring[ringslot][:, :], ACT.Copy).then_inc(hi_done, 1)

        def expert0_high(act, j):
            slot = EXPERT_SLOT[j]
            high_of(act, slot, 16 * (PRO_USES[slot] + 1), LEAD + j + 1, (LEAD + j) % SPLITS)

        def low_of(dve, ringslot, count, parts):
            dve.wait_ge(hi_done, count)
            dve.wait_ge(chunk_used, count - SPLITS)
            nc.vector.tensor_tensor(w_lo[parts][:, :], ring[ringslot][:, :],
                                    w_hi[parts][:, :].bitcast(F32), ALU.subtract).then_inc(lo_done, 1)

        def second_load(sp, m):
            sp.wait_ge(lo_done, LEAD + m + 1)
            sp.dma_start(ring[EXPERT_SLOT[m]][:, :], stream[N_PRO + PER_EXPERT + m, :, :]
                         ).then_inc(w_loaded[EXPERT_SLOT[m]], 16)

        def moe_sync(sp):
            def first_load(m):
                sp.dma_start(ring[EXPERT_SLOT[m]][:, :], stream[N_PRO + m, :, :]
                             ).then_inc(w_loaded[EXPERT_SLOT[m]], 16)

            sp.wait_ge(u_stored[0], 32)
            first_load(SLOTS - 1)
            for t in range(TT):
                sp.wait_ge(acc_made, t + 1)
                sp.dma_start(acc_dram[t * P:(t + 1) * P, :], h[:, t, :]).then_inc(acc_stored[t // 2], 16)
            for i in range(2):
                sp.wait_ge(acc_stored[i], 32)
                first_load(PRO_SLOTS + i)
            for m in range(EARLY, PER_EXPERT):
                second_load(sp, m)

            def rounds(first, base):
                with sp.Fori(first, E) as r:
                    for m in range(PER_EXPERT):
                        slot = EXPERT_SLOT[m]
                        sp.wait_ge(lo_done, (r + base) * PER_EXPERT + (LEAD - PER_EXPERT + m + 1))
                        sp.dma_start(ring[slot][:, :], stream[bass.ds(r * PER_EXPERT + (N_PRO + m), 1),
                                                              :, :]
                                     .rearrange("o p c -> (o p) c")).then_inc(w_loaded[slot], 16)

            rounds(2, 0)
            sp.wait_ge(count_made, 1)
            most = sp.value_load(n_max_u[0:1, 0:1], min_val=0, max_val=T)
            with sp.Fori(1, TT) as b:
                with sp.If(most > b * P):
                    rounds(0, b * E)
            sp.wait_ge(moe_over, 1)
            for t in range(TT):
                sp.dma_start(fin[t][:, :], acc_dram[t * P:(t + 1) * P, :]).then_inc(fin_loaded[t], 16)
                if t == 0:
                    sp.dma_start(fin_g[:, :], norm_final_g.partition_broadcast(P)
                                 ).then_inc(acc_loaded, 16)
            for t in range(TT):
                sp.wait_ge(fin_made, t + 1)
                sp.dma_start(out[t * P:(t + 1) * P, :], fin[t][:, :]).then_inc(out_stored, 16)
            sp.wait_ge(out_stored, 16 * TT)

        def moe_pool(pool):
            G = nc.gpsimd
            pool.wait_ge(h_mean, 1)
            G.tensor_tensor(rms2[:, :], rms2[:, :], power[:, 0:TT], ALU.pow).then_inc(h_rms, 1)

            for t in (2, 3):
                if t == 2:
                    pool.wait_ge(h_rms, 1)
                else:
                    pool.wait_ge(u_late, 1)
                pool.wait_ge(u_scaled, t - 1)
                G.tensor_tensor(u2[t][:, :], u2[t][:, :], ffn_g[:, :], ALU.mult).then_inc(u_late, 1)
            pool.wait_ge(u_late, 2)
            pool.wait_ge(b1_hi_done, 1)
            G.tensor_tensor(b1_hl[E:2 * E, :], b1_raw[E:2 * E, :], b1_hl[E:2 * E, :].bitcast(F32),
                            ALU.subtract).then_inc(b1_lo_done, 1)
            pool.wait_ge(b1_lo_done, 1)

            def gather(e, g):
                pool.wait_ge(slot_info, g + 1)
                if e >= 2:
                    pool.wait_ge(xt_ps, 2 * (g - 1))
                G.indirect_dma_start(
                    out=xe[e % 2][:, :], out_offset=None, in_=u_dram[:, :],
                    in_offset=bass.IndirectOffsetOnAxis(ap=slot_token[:, e:e + 1], axis=0),
                    bounds_check=T - 1).then_inc(xe_loaded[e % 2], 16)

            def scatter(e, g):
                pool.wait_ge(y_made_half, 2 * g + 2)
                if g:
                    pool.wait_ge(scattered, 16 * g)
                G.indirect_dma_start(
                    out=acc_dram[:, :],
                    out_offset=bass.IndirectOffsetOnAxis(ap=slot_row[:, e:e + 1], axis=0),
                    in_=y_sb[e % 2][:, :], in_offset=None, bounds_check=T + P - 1,
                    compute_op=ALU.add).then_inc(scattered, 16)

            def a_pass(base):
                gather(0, base)
                gather(1, base + 1)
                if base == 0:
                    for i in range(2):
                        pool.wait_ge(acc_stored[i], 32)
                    pool.wait_ge(trash_stored, 16)
                for e in range(E):
                    if e + 2 < E:
                        gather(e + 2, base + e + 2)
                    scatter(e, base + e)
                pool.wait_ge(scattered, 16 * (base + E))

            for i in range(2):
                pool.wait_ge(u_stored[i], 16 * TT // 2)
            a_pass(0)
            pool.wait_ge(count_made, 1)
            most = pool.value_load(n_max_u[0:1, 0:1], min_val=0, max_val=T)
            for b in range(1, TT):
                with pool.If(most > b * P):
                    a_pass(b * E)
            G.memset(power[:, :], -0.5).then_inc(moe_over, 1)
            for t in range(TT):
                pool.wait_ge(fin_mean, t + 1)
                G.tensor_tensor(fin_rms_t[:, t:t + 1], fin_rms_t[:, t:t + 1], power[:, 0:1], ALU.pow
                                ).then_inc(fin_rms, 1)

        def moe_act(act):
            A_ = nc.scalar.activation

            def high(j, g):
                slot, uses, parts = chunk_slot(j)
                high_of(act, slot, g * 16 + 16 * (uses + 1), g * PER_EXPERT + (IT + j + 1), parts)

            def x_part(g, par, i, at=XT):
                act.wait_ge(xt_ps, g * 2 + i + 1)
                A_(xe_hi[par][:, 4 * i:4 * i + 4, :].rearrange("p k s -> p (k s)"), bank[at], ACT.Copy
                   ).then_inc(xt_hi_made, 1)

            def sigmoid(g, half):
                act.wait_ge(glu_made, g * 2 + half + 1)
                if later(g) or half:
                    act.wait_ge(hid_made, g * 2 + half)
                A_(sig[:, :], glu[:, :], ACT.Sigmoid, scale=1.702).then_inc(sig_made, 1)

            def hid_part(g, half):
                act.wait_ge(hid_t_ps, g * 2 + half + 1)
                A_(hid_hi[half][:, :, :].rearrange("p f s -> p (f s)"), bank[HT], ACT.Copy
                   ).then_inc(hid_hi_made, 1)

            def outputs(e, g, par, count):
                act.wait_ge(chunk_used, count)
                if later(g):
                    act.wait_ge(scattered, 16 * g)
                for i in range(2):
                    A_(y_sb[par][:, 512 * i:512 * i + 512], bank[Y0 + i], ACT.Copy,
                       scale=slot_gate[:, bass.ds(e, 1)]).then_inc(y_made_half, 1)

            def iteration(e, g, par, last):
                high(3, g)
                hid_part(g, 0)
                high(4, g)
                high(5, g)
                if not last:
                    x_part(g + 1, 1 - par, 0)
                high(6, g)
                sigmoid(g, 1)
                if not last:
                    x_part(g + 1, 1 - par, 1)
                high(7, g)
                if not last:
                    high(8, g)
                    high(9, g)
                hid_part(g, 1)
                if not last:
                    high(10, g)
                    high(11, g)
                    high(12, g)
                    sigmoid(g + 1, 0)
                    high(13, g)
                    high(14, g)
                outputs(e, g, par, g * PER_EXPERT + (IT + (8 if last else 12)))

            def a_pass(base, first):
                for j in range(EARLY * first, 4):
                    c = LEAD + j
                    if j == EARLY:
                        x_part(base, 0, 0)
                        x_part(base, 0, 1, HT)
                    high_of(act, EXPERT_SLOT[j], base * 16 + 16 * (PRO_USES[EXPERT_SLOT[j]] + 1),
                            base * PER_EXPERT + (c + 1), c % SPLITS)
                high(0, base)
                sigmoid(base, 0)
                high(1, base)
                high(2, base)
                for par in range(2 * first):
                    iteration(par, par, par, False)
                with act.Fori(first, PAIRS - 1) as i:
                    for par in range(2):
                        iteration(i * 2 + par, i * 2 + (base + par), par, False)
                for par in range(2):
                    iteration(E - 2 + par, base + (E - 2 + par), par, par == 1)

            a_pass(0, 1)
            act.wait_ge(count_made, 1)
            most = act.value_load(n_max_u[0:1, 0:1], min_val=0, max_val=T)
            with act.Fori(1, TT) as b:
                with act.If(most > b * P):
                    a_pass(b * E, 0)
            for t in range(TT):
                act.wait_ge(fin_loaded[t], 16)
                if t:
                    act.wait_ge(fin_ssq, t)
                A_(fin_junk[:, :], fin[t][:, :], ACT.Square, accum_out=fin_ssq_t[:, t:t + 1]
                   ).then_inc(fin_ssq, 1)

        def moe_dve(dve):
            V = nc.vector
            f = lambda a: a.bitcast(F32)

            def low(j, g):
                slot, _, parts = chunk_slot(j)
                low_of(dve, slot, g * PER_EXPERT + (IT + j + 1), parts)

            def slot_masks(e, g):
                if later(g):
                    dve.wait_ge(slot_ps, g)
                for t in range(TT):
                    ins = V.tensor_scalar(onehot[:, t, :], const["slots"], pos[:, t, bass.ds(e, 1)],
                                          None, ALU.is_equal)
                ins.then_inc(onehot_made, 1)

            def select(e, par):
                V.tensor_copy(sel[par][:, :], const["rows2e"][0:2 * E, bass.ds(e, 1)]
                              .to_broadcast([2 * E, P])).then_inc(sel_made, 1)

            def slot_scalars(e, g):
                dve.wait_ge(slot_ps, g + 1)
                V.tensor_copy(slot_token[:, bass.ds(e, 1)], bank[XT][:, 0:1]).then_inc(slot_parts, 1)
                V.tensor_copy(slot_gate[:, bass.ds(e, 1)], bank[XT][:, 1:2]).then_inc(slot_parts, 1)
                V.tensor_scalar(valid[:, :], bank[XT][:, 2:3], -1.0, 1.0, ALU.mult, ALU.add
                                ).then_inc(slot_parts, 1)
                dve.wait_ge(slot_parts, g * 3 + 3)
                V.scalar_tensor_tensor(slot_row[:, bass.ds(e, 1)], const["trash"], valid[:, 0:1],
                                       bank[XT][:, 0:1], ALU.mult, ALU.add).then_inc(slot_info, 1)

            def x_part(g, par, i, at=XT):
                dve.wait_ge(xt_hi_made, g * 2 + i + 1)
                V.tensor_tensor(xe_lo[par][:, 4 * i:4 * i + 4, :].rearrange("p k s -> p (k s)"),
                                bank[at], f(xe_hi[par][:, 4 * i:4 * i + 4, :]
                                            .rearrange("p k s -> p (k s)")), ALU.subtract
                                ).then_inc(xt_lo_made, 1)

            def clamp(g, half, count):
                dve.wait_ge(chunk_used, count)
                if later(g) or half:
                    dve.wait_ge(hid_t_ps, g * 2 + half)
                V.tensor_scalar(glu[:, :], bank[GLU[half]], 7.0, None, ALU.min).then_inc(glu_made, 1)
                V.tensor_scalar(lin[:, :], bank[LINEAR[half]], 7.0, -7.0, ALU.min, ALU.max
                                ).then_inc(lin_made, 1)

            def hidden(g, half):
                dve.wait_ge(lin_made, g * 2 + half + 1)
                V.scalar_tensor_tensor(lin[:, :], lin[:, :], 1.0, glu[:, :], ALU.add, ALU.mult
                                       ).then_inc(u_half, 1)
                dve.wait_ge(u_half, g * 2 + half + 1)
                dve.wait_ge(sig_made, g * 2 + half + 1)
                V.tensor_tensor(lin[:, :], lin[:, :], sig[:, :], ALU.mult).then_inc(hid_made, 1)

            def hid_part(g, half):
                dve.wait_ge(hid_hi_made, g * 2 + half + 1)
                V.tensor_tensor(hid_lo[half][:, :, :].rearrange("p f s -> p (f s)"), bank[HT],
                                f(hid_hi[half][:, :, :].rearrange("p f s -> p (f s)")), ALU.subtract
                                ).then_inc(hid_lo_made, 1)

            def iteration(e, g, par, last, far):
                low(3, g)
                hid_part(g, 0)
                if far:
                    slot_masks(e + 2, g + 2)
                low(4, g)
                if not last:
                    select(e + 1, 1 - par)
                low(5, g)
                if not last:
                    x_part(g + 1, 1 - par, 0)
                clamp(g, 1, g * PER_EXPERT + (IT + 4))
                if last:
                    hidden(g, 1)
                low(6, g)
                if last:
                    hid_part(g, 1)
                else:
                    x_part(g + 1, 1 - par, 1)
                    hidden(g, 1)
                low(7, g)
                if not last:
                    low(8, g)
                    if far:
                        slot_scalars(e + 2, g + 2)
                    low(9, g)
                    hid_part(g, 1)
                    low(10, g)
                    low(11, g)
                    clamp(g + 1, 0, g * PER_EXPERT + (IT + 10))
                    low(12, g)
                    hidden(g + 1, 0)
                    low(13, g)
                    low(14, g)

            def constants(t0):
                for t in range(t0, t0 + 2):
                    dve.wait_ge(b2_ps, t + 1)
                    b = 2 * (t % 2)
                    dst = h[:, t, :].rearrange("p (n c) -> p n c", n=2)
                    V.tensor_tensor(dst, dst, psum[:, b:b + 2, :], ALU.add).then_inc(acc_made, 1)

            def a_pass(base, first):
                for e in range(2):
                    slot_masks(e, base + e)
                    if first and e == 0:
                        dve.wait_ge(gates_hi_made, 1)
                        V.tensor_tensor(gates_hl[E:2 * E, :], bank[6][E:2 * E, :],
                                        f(gates_hl[E:2 * E, :]), ALU.subtract).then_inc(gates_t_made, 1)
                    if first and e == 1:
                        constants(0)
                    slot_scalars(e, base + e)
                if first:
                    constants(2)
                select(0, 0)
                for j in range(EARLY * first, 4):
                    c = LEAD + j
                    if j == max(2, EARLY * first):
                        x_part(base, 0, 0)
                        x_part(base, 0, 1, HT)
                    low_of(dve, EXPERT_SLOT[j], base * PER_EXPERT + (c + 1), c % SPLITS)
                low(0, base)
                clamp(base, 0, base * PER_EXPERT + (LEAD + 4))
                hidden(base, 0)
                low(1, base)
                low(2, base)
                for par in range(2 * first):
                    iteration(par, par, par, False, True)
                with dve.Fori(first, PAIRS - 1) as i:
                    for par in range(2):
                        iteration(i * 2 + par, i * 2 + (base + par), par, False, True)
                for par in range(2):
                    iteration(E - 2 + par, base + (E - 2 + par), par, par == 1, False)

            dve.wait_ge(pos_made, 1)
            a_pass(0, 1)
            dve.wait_ge(count_made, 1)
            most = dve.value_load(n_max_u[0:1, 0:1], min_val=0, max_val=T)
            with dve.Fori(1, TT) as b:
                with dve.If(most > b * P):
                    V.tensor_scalar(pos[:, :, :], pos[:, :, :], -float(P), None, ALU.add
                                    ).then_inc(pos_shifted, 1)
                    dve.wait_ge(pos_shifted, b)
                    a_pass(b * E, 0)
            dve.wait_ge(acc_loaded, 16)
            for t in range(TT):
                dve.wait_ge(fin_ssq, t + 1)
                V.tensor_scalar(fin_rms_t[:, t:t + 1], fin_ssq_t[:, t:t + 1], 1.0 / D, EPS, ALU.mult,
                                ALU.add).then_inc(fin_mean, 1)
                dve.wait_ge(fin_rms, t + 1)
                V.scalar_tensor_tensor(fin[t][:, :], fin[t][:, :], fin_rms_t[:, t:t + 1], fin_g[:, :],
                                       ALU.mult, ALU.mult).then_inc(fin_made, 1)

        def moe_pe(pe):
            MM = nc.tensor.matmul

            def products(count, parts, outs, xh, xl, k0, width, first, last):
                wh = w_hi[parts][:, :].rearrange("p (k c) -> p k c", k=2)
                wl = w_lo[parts][:, :].rearrange("p (k c) -> p k c", k=2)
                pe.wait_ge(hi_done, count)
                for i in range(2):
                    for n in range(2):
                        cols = slice(512 * n, 512 * n + 512)
                        MM(outs[n], xh[:, k0 + i, :], wh[:, i, cols], start=(first and i == 0), stop=False)
                        MM(outs[n], xl[:, k0 + i, :], wh[:, i, cols], start=False, stop=False)
                pe.wait_ge(lo_done, count)
                for i in range(2):
                    for n in range(2):
                        cols = slice(512 * n, 512 * n + 512)
                        ins = MM(outs[n], xh[:, k0 + i, :], wl[:, i, cols], start=False,
                                 stop=(last and i == 1))
                ins.then_inc(chunk_used, 1)

            def w1_chunk(count, parts, half, par, k0, g):
                if k0 == DK - 2:
                    pe.wait_ge(sel_made, g + 1)
                    for n, b in enumerate((GLU[half], LINEAR[half])):
                        c0 = D * n + 512 * half
                        MM(bank[b], sel[par][:, :], b1_hl[:, c0:c0 + 512], start=False, stop=False)
                products(count, parts, (bank[GLU[half]], bank[LINEAR[half]]), xe_hi[par], xe_lo[par],
                         k0, 512, k0 == 0, k0 == DK - 2)

            def w2_chunk(count, parts, half, f0):
                products(count, parts, (bank[Y0], bank[Y0 + 1]), hid_hi[half], hid_lo[half], f0, 512,
                         half == 0 and f0 == 0, half == 1 and f0 == 2)

            def slots(e, g):
                pe.wait_ge(onehot_made, g + 1)
                for t in range(TT):
                    ins = MM(bank[XT][:, 0:4], onehot[:, t, :],
                             slot_rhs[:, t, bass.ds(e, 1), :].rearrange("p o j -> p (o j)"),
                             start=(t == 0), stop=(t == TT - 1))
                ins.then_inc(slot_ps, 1)

            def turn_x(g, pair, par, i, to):
                if i == 0:
                    pe.wait_ge(xe_loaded[par], pair * 16 + 16)
                elif to == XT:
                    pe.wait_ge(xt_lo_made, g * 2 + 1)
                for k in range(4):
                    ins = nc.tensor.transpose(bank[to][:, P * k:P * k + P],
                                              xe[par][:, P * (4 * i + k):P * (4 * i + k) + P], ident)
                ins.then_inc(xt_ps, 1)

            def turn_hid(g, half):
                pe.wait_ge(hid_made, g * 2 + half + 1)
                for k in range(4):
                    ins = nc.tensor.transpose(bank[HT][:, P * k:P * k + P], lin[:, P * k:P * k + P],
                                              ident)
                ins.then_inc(hid_t_ps, 1)

            def iteration(e, g, pair, par, last, far):
                def count(j):
                    return g * PER_EXPERT + (IT + j + 1)

                parts = lambda j: chunk_slot(j)[2]
                if later(g):
                    pe.wait_ge(lin_made, g * 2)
                for j in range(4):
                    w1_chunk(count(j), parts(j), 1, par, 2 * j, g)
                    if j == 1:
                        turn_hid(g, 0)
                if not last:
                    pe.wait_ge(slot_info, g + 2)
                    turn_x(g + 1, pair + par, 1 - par, 0, XT)
                if later(g):
                    pe.wait_ge(y_made_half, g * 2)
                pe.wait_ge(hid_lo_made, g * 2 + 1)
                w2_chunk(count(4), parts(4), 0, 0)
                if not last:
                    turn_x(g + 1, pair + par, 1 - par, 1, XT)
                w2_chunk(count(5), parts(5), 0, 2)
                j = 6
                if not last:
                    pe.wait_ge(lin_made, g * 2 + 1)
                    pe.wait_ge(xt_lo_made, g * 2 + 4)
                    for j in range(6, 10):
                        w1_chunk(count(j), parts(j), 0, 1 - par, 2 * (j - 6), g + 1)
                        if j == 6 and far:
                            slots(e + 2, g + 2)
                        if j == 7:
                            turn_hid(g, 1)
                    j = 10
                else:
                    turn_hid(g, 1)
                pe.wait_ge(hid_lo_made, g * 2 + 2)
                w2_chunk(count(j), parts(j), 1, 0)
                w2_chunk(count(j + 1), parts(j + 1), 1, 2)

            def constants(t0):
                for t in range(t0, t0 + 2):
                    if t >= 2:
                        pe.wait_ge(acc_made, t - 1)
                    for n in range(2):
                        ins = MM(bank[2 * (t % 2) + n], gates_hl[:, P * t:P * t + P],
                                 b2_hl[:, 512 * n:512 * n + 512], start=True, stop=True)
                    ins.then_inc(b2_ps, 1)

            def a_pass(base, pair0, first):
                slots(0, base)
                if first:
                    pe.wait_ge(b2_lo_done, 1)
                    pe.wait_ge(gates_t_made, 1)
                    constants(0)
                pe.wait_ge(slot_info, base + 1)
                slots(1, base + 1)
                if first:
                    constants(2)
                pe.wait_ge(slot_info, base + 2)
                turn_x(base, pair0, 0, 0, XT)
                turn_x(base, pair0, 0, 1, HT)
                if first:
                    pe.wait_ge(acc_made, TT)
                else:
                    pe.wait_ge(lin_made, base * 2)
                pe.wait_ge(xt_lo_made, base * 2 + 1)
                for j in range(4):
                    if j == 2:
                        pe.wait_ge(xt_lo_made, base * 2 + 2)
                    if j == 3 and first:
                        pe.wait_ge(b1_lo_done, 1)
                    w1_chunk(base * PER_EXPERT + (LEAD + j + 1), (LEAD + j) % SPLITS, 0, 0, 2 * j, base)
                for par in range(2 * first):
                    iteration(par, par, 0, par, False, True)
                with pe.Fori(first, PAIRS - 1) as i:
                    for par in range(2):
                        iteration(i * 2 + par, i * 2 + (base + par), i + pair0, par, False, True)
                for par in range(2):
                    iteration(E - 2 + par, base + (E - 2 + par), pair0 + (PAIRS - 1), par, par == 1,
                              False)

            pe.wait_ge(pos_made, 1)
            a_pass(0, 0, 1)
            pe.wait_ge(count_made, 1)
            most = pe.value_load(n_max_u[0:1, 0:1], min_val=0, max_val=T)
            with pe.Fori(1, TT) as b:
                with pe.If(most > b * P):
                    a_pass(b * E, b * PAIRS, 0)

        @block.sync
        def _(sp):
            def load_chunk(slot, n):
                sp.dma_start(ring[slot][:, :], stream[n, :, :]).then_inc(w_loaded[slot], 16)

            sp.dma_start(vec[:, :], vectors[:, :]).then_inc(vec_loaded, 16)
            for n in (0, N_X, 1):
                load_chunk(n, n)
            sp.dma_start(main[:, :], consts[:, 0:main_w]).then_inc(const_loaded, 16)
            sp.dma_start(wdt[:, :, :], w_dt[:, :, :]).then_inc(const_loaded, 16)
            bw = main_w + 2 * P
            sp.dma_start(band[:, 0:FW], consts[0:BUCKETS + 1, bw:bw + FW]).then_inc(const_loaded, 16)
            sp.dma_start(rel[0:BUCKETS, :], rel_bias[:, :]).then_inc(const_loaded, 16)
            sp.dma_start(rel[BUCKETS:BUCKETS + 1, :],
                         consts[0:1, bw + FW:bw + FW + HEADS]).then_inc(const_loaded, 16)
            for n in range(N_X + 1, PRO_SLOTS):
                load_chunk(n, n)
            sp.wait_ge(band_made, 1)
            sp.dma_start(bass.AP(band_dram, 0, [[FW, HEADS], [HEADS * FW, P], [1, FW]]),
                         band_rows[:, 0:FW].rearrange("h (o f) -> h o f", o=1)
                         .to_broadcast([HEADS, P, FW])).then_inc(band_stored, 16)
            for n in range(PRO_SLOTS, N_PRO):
                if n < PRO_SLOTS + N_X:
                    sp.wait_ge(xg_lo_done, 4 * (n - PRO_SLOTS + 1))
                    sp.wait_ge(sq_done, n - PRO_SLOTS + 1)
                else:
                    sp.wait_ge(lo_done, n - PRO_SLOTS - N_X + 1)
                load_chunk(n % PRO_SLOTS, n)
            for m in range(5):
                if m == 1:
                    sp.wait_ge(dt_ps, 1)
                    sp.dma_start(incl[:, :], consts[:, main_w:main_w + P]).then_inc(incl_loaded, 16)
                sp.wait_ge(lo_done, 5 + m)
                load_chunk(EXPERT_SLOT[m], N_PRO + m)
            sp.wait_ge(chunk_used, N_IN)
            sp.dma_start(negmask[:, :], consts[:, main_w + P:main_w + 2 * P]
                         ).then_inc(scan_consts_loaded, 16)
            sp.wait_ge(silu_done, 8)
            sp.wait_ge(band_stored, 16)
            sp.dma_start(bias[:, :, :], bass.AP(band_dram, P - 1, [[HEADS * FW - 1, P], [FW, HEADS],
                                                                   [1, 2 * P]])
                         ).then_inc(bias_loaded, 16)
            sp.dma_start(h[:, :, :], x.rearrange("(t p) d -> p t d", p=P)).then_inc(h_loaded, 16)
            sp.wait_ge(h_loaded, 16)
            sp.dma_start(acc_dram[T:T + P, :], h[:, 0, :]).then_inc(trash_stored, 16)
            sp.wait_ge(mix_ps, 1)
            sp.dma_start(ffn_g[:, :], norm_ffn_g.partition_broadcast(P)).then_inc(router_loaded, 16)
            sp.dma_start(wr[:, :, :], w_router.rearrange("(k p) e -> p k e", p=P)
                         ).then_inc(router_loaded, 16)
            for i in range(3):
                sp.dma_start(b2_sb[E * i:E * i + E, :], b2[:, :]).then_inc(router_loaded, 16)
            for m in range(5, PRO_SLOTS):
                sp.wait_ge(lo_done, 5 + m)
                load_chunk(EXPERT_SLOT[m], N_PRO + m)
            for m in range(EARLY - 1):
                second_load(sp, m)
            sp.wait_ge(chunk_used, N_IN + N_OUT)
            sp.dma_start(b1_raw[0:E, :], b1[:, :]).then_inc(b1_loaded, 16)
            sp.dma_start(b1_raw[E:2 * E, :], b1[:, :]).then_inc(b1_loaded, 16)
            second_load(sp, EARLY - 1)
            for t in range(TT):
                if t < 2:
                    sp.wait_ge(u_made, t + 1)
                else:
                    sp.wait_ge(u_late, t - 1)
                sp.dma_start(u_dram[t * P:(t + 1) * P, :], u2[t][:, :]).then_inc(u_stored[t // 2], 16)
            moe_sync(sp)

        @block.gpsimd
        def _(pool):
            nc.gpsimd.memset(conv_in[:, :, 0:4], 0.0).then_inc(pads_made, 1)
            nc.gpsimd.memset(k_t[:, 0:P], 0.0).then_inc(pads_made, 1)
            nc.gpsimd.memset(v_tok[:, 0, :], 0.0).then_inc(pads_made, 1)
            nc.gpsimd.memset(slot_rhs[:, :, :, 2], 1.0).then_inc(rhs_filled, 1)
            nc.gpsimd.memset(slot_rhs[:, :, :, 3], 0.0).then_inc(rhs_filled, 1)
            pool.wait_ge(const_loaded, 80)
            nc.gpsimd.tensor_copy(slot_rhs[:, :, :, 0], const["tokens"].rearrange("p (t o) -> p t o", o=1)
                                  .to_broadcast([P, TT, E])).then_inc(rhs_filled, 1)
            nc.gpsimd.memset(power[:, :], -0.5).then_inc(rhs_filled, 1)

            def inverse_root(c):
                pool.wait_ge(mean_made, c + 1)
                pool.wait_ge(rhs_filled, 4)
                nc.gpsimd.tensor_tensor(rms[:, 2 * c:2 * c + 2], rms[:, 2 * c:2 * c + 2],
                                        power[:, 0:2], ALU.pow).then_inc(rms_made, 1)

            pool.wait_ge(cum_exp, 3)
            for c in range(TT):
                pool.wait_ge(tok_made, 2 * c + 1)
                if c:
                    pool.wait_ge(y_ps, c)
                    pool.wait_ge(y_read, c)
                xt = x_toks[c % 2][:, :].rearrange("p (h d) -> p h d", h=HEADS)

                def per_head(a):
                    return a.rearrange("p (h o) -> p h o", o=1).to_broadcast([P, HEADS, HD])

                o3 = lambda a: a[:, :].rearrange("p (h d) -> p h d", h=HEADS)
                nc.gpsimd.tensor_tensor(o3(xdt), xt, per_head(dt[:, 8 * c:8 * c + 8]), ALU.mult
                                        ).then_inc(xs_made, 1)
                pool.wait_ge(xs_made, 3 * c + 1)
                nc.gpsimd.tensor_tensor(o3(xdd), o3(xdt), per_head(dend[:, 8 * c:8 * c + 8]),
                                        ALU.mult).then_inc(xs_made, 1)
                nc.gpsimd.tensor_tensor(o3(xskip), xt, per_head(v["d_skip"]), ALU.mult
                                        ).then_inc(xs_made, 1)
                if c:
                    inverse_root(c - 1)
            inverse_root(TT - 1)
            moe_pool(pool)

        @block.scalar
        def _(act):
            A_ = nc.scalar.activation
            act.wait_ge(vec_loaded, 16)
            def high(c):
                n = c + N_X
                slot = n % PRO_SLOTS
                act.wait_ge(w_loaded[slot], 16 * (n // PRO_SLOTS + 1))
                if c >= SPLITS:
                    act.wait_ge(chunk_used, c - SPLITS + 1)
                A_(w_hi[c % SPLITS][:, :], ring[slot][:, :], ACT.Copy).then_inc(hi_done, 1)

            def after_proj(c):
                if c < N_XBC:
                    for i in silu_tiles(c):
                        if i == 0:
                            act.wait_ge(band_stored, 16)
                        act.wait_ge(conv_done, i + 1)
                        A_(xbc[:, i, :], conv_acc[:, i % 2, :], ACT.Silu).then_inc(silu_done, 1)
                elif c < N_XBC + N_Z:
                    half = c - N_XBC
                    act.wait_ge(chunk_used, c + 1)
                    act.wait_ge(rstd_tok_made, 1)
                    act.wait_ge(ss_ps, 1)
                    for t in range(TT):
                        b = 2 * (c % 3) + t // 2
                        A_(zs[:, t, 256 * half:256 * half + 256],
                           bank[b][:, 256 * (t % 2):256 * (t % 2) + 256], ACT.Silu,
                           scale=rstd_tok[:, t:t + 1]).then_inc(z_made, 1)
                elif c == N_XBC + N_Z:
                    act.wait_ge(chunk_used, c + 1)
                    for t in range(TT):
                        A_(v_tok[:, t + 1, :], bank[2 * (c % 3) + 1][:, P * t:P * t + P], ACT.Copy,
                           scale=rstd_tok[:, t:t + 1]).then_inc(v_made, 1)

            for n in range(N_X):
                act.wait_ge(w_loaded[n], 16)
                for j in range(4):
                    k = 4 * n + j
                    A_(xg_hi[:, k, :], ring[n][:, j * T:(j + 1) * T], ACT.Copy,
                       scale=v["norm_mix_g"][:, k:k + 1]).then_inc(xg_hi_done, 1)
                if n == 0:
                    high(0)
            for n in range(N_X):
                A_(sq[:, 4 * n:4 * n + 4, :].rearrange("p k t -> p (k t)"), ring[n][:, :], ACT.Square
                   ).then_inc(sq_done, 1)
            high(1)
            high(2)
            act.wait_ge(const_loaded, 80)
            A_(wdt_hi[:, :, :], wdt[:, :, :], ACT.Copy).then_inc(wdt_hi_done, 1)
            act.wait_ge(ms_made, 1)
            A_(rstd_row[:, :], rstd_row[:, :], ACT.Sqrt).then_inc(rms_root, 1)
            for c in range(3, N_IN):
                high(c)
                if c <= 6:
                    after_proj(c - 3)
                if c >= 6:
                    after_proj(c - 2)

            act.wait_ge(dt_arg, 1)
            A_(dt_e[:, :], dt_e[:, :], ACT.Exp, scale=-1.0).then_inc(dt_exp, 1)
            A_(a_neg[:, :], v["a_log"], ACT.Exp).then_inc(a_exp, 1)
            act.wait_ge(dt_one, 1)
            A_(dt_l[:, :], dt_u[:, :], ACT.Ln).then_inc(dt_log, 1)
            act.wait_ge(cum_made, 3)
            A_(eacum[:, :], acum[:, :], ACT.Exp).then_inc(cum_exp, 1)
            A_(dtot[:, :], dtot[:, :], ACT.Exp).then_inc(cum_exp, 1)
            A_(dend[:, :], dend[:, :], ACT.Exp).then_inc(cum_exp, 1)
            act.wait_ge(scan_consts_loaded, 16)
            A_(negmask_r[:, :], negmask[:, :], ACT.Copy).then_inc(mask_rounded, 1)
            A_(ident_r[:, :], ident, ACT.Copy).then_inc(mask_rounded, 1)

            def exps(a):
                lo = P if a // 4 == 0 else 0
                act.wait_ge(nmax_made, a + 1)
                if a >= 2:
                    act.wait_ge(pt_ps, a - 1)
                for i in range(2):
                    A_(probs[a % 2][:, i, lo:], scores[a % 2][:, i, lo:], ACT.Exp,
                       bias=nmax[:, 2 * a + i:2 * a + i + 1],
                       accum_out=psums[:, 2 * a + i:2 * a + i + 1]).then_inc(exp_made, 1)
                A_(esink[:, 2 * a:2 * a + 2], sinkd[:, 2 * a:2 * a + 2], ACT.Exp).then_inc(exp_made, 1)

            def scan(c, q):
                if q == 0:
                    act.wait_ge(tok_ps, c + 1)
                    if c >= 2:
                        act.wait_ge(xs_made, 3 * (c - 1))
                    A_(x_toks[c % 2][:, :], bank[0][:, :], ACT.Copy).then_inc(tok_made, 1)
                    A_(b_toks[c % 2][:, :, :].rearrange("p g n -> p (g n)"), bank[1][:, 0:256],
                       ACT.Copy).then_inc(tok_made, 1)
                elif q in (1, 2):
                    g = q - 1
                    act.wait_ge(bc_ps, 2 * c + g + 1)
                    if c:
                        act.wait_ge(m_made, 2 * c - 1 + g)
                    for r in range(4):
                        j = 8 * c + 4 * g + r
                        A_(decay[g][:, r, :], bank[2][:, P * r:P * r + P], ACT.Exp,
                           bias=nacum[:, j:j + 1]).then_inc(decay_made, 1)

            def squares_of(c):
                act.wait_ge(o_read, 4 * c + 4)
                act.wait_ge(y_read, c + 1)
                for i in range(2):
                    if 2 * c + i:
                        act.wait_ge(ssq_made, 2 * c + i)
                    A_(sq_junk[:, :], mix[:, c, 512 * i:512 * i + 512], ACT.Square,
                       accum_out=ssq[:, 2 * c + i:2 * c + i + 1]).then_inc(ssq_made, 1)

            def norm(c):
                act.wait_ge(rms_made, c + 1)
                for i in range(2):
                    A_(mix[:, c, 512 * i:512 * i + 512], mix[:, c, 512 * i:512 * i + 512], ACT.Copy,
                       scale=rms[:, 2 * c + i:2 * c + i + 1]).then_inc(normed, 1)

            exps(0)
            exps(1)
            for a in range(16):
                c, q = a // 4, a % 4
                act.wait_ge(pt_ps, a + 1)
                if a >= 2:
                    act.wait_ge(o_ps, a - 1)
                lo = 2 if c == 0 else 0
                if c == 0:
                    A_(probs_t[a % 2][:, 2:4, :].rearrange("p a b -> p (a b)"), bank[6][:, 256:512],
                       ACT.Copy).then_inc(pt_made, 1)
                else:
                    A_(probs_t[a % 2][:, :, :].rearrange("p a b -> p (a b)"), bank[6][:, :],
                       ACT.Copy).then_inc(pt_made, 1)
                scan(c, q)
                if a + 2 < 16:
                    exps(a + 2)
                if q == 1 and c:
                    squares_of(c - 1)
                if q == 2 and c:
                    norm(c - 1)
            act.wait_ge(y_ps, TT)
            act.wait_ge(xs_made, 3 * TT)
            high(N_IN)
            squares_of(TT - 1)
            norm(TT - 1)

            for k in range(DK):
                act.wait_ge(mix_ps, k + 1)
                A_(mix_hi[:, k, :], bank[k][:, :], ACT.Copy, scale=v["mix_g"][:, k:k + 1]
                   ).then_inc(mix_hi_done, 1)
            for c in range(N_IN + 1, N_IN + N_OUT):
                high(c)
            router_act(act)
            moe_act(act)

        @block.vector
        def _(dve):
            V = nc.vector
            steps = [0]

            def step(ins):
                steps[0] += 1
                ins.then_inc(dve_step, 1)
                dve.wait_ge(dve_step, steps[0])

            def mark(ins):
                steps[0] += 1
                ins.then_inc(dve_step, 1)

            f = lambda a: a.bitcast(F32)
            dve.wait_ge(vec_loaded, 16)
            def low(c):
                n = c + N_X
                slot = n % PRO_SLOTS
                dve.wait_ge(hi_done, c + 1)
                if c >= SPLITS:
                    dve.wait_ge(chunk_used, c - SPLITS + 1)
                V.tensor_tensor(w_lo[c % SPLITS][:, :], ring[slot][:, :], f(w_hi[c % SPLITS][:, :]),
                                ALU.subtract).then_inc(lo_done, 1)

            evacs = [0]

            def evac(dst, src):
                V.tensor_tensor(dst, src, rstd_row[:, :], ALU.mult).then_inc(proj_evac, 1)
                evacs[0] += 1

            def after_proj(c):
                b = 2 * (c % 3)
                if c < N_XBC:
                    dve.wait_ge(chunk_used, c + 1)
                    for i, tile in enumerate(silu_tiles(c)):
                        evac(conv_in[:, tile % 2, 3:3 + T], bank[b + i][:, :])
                        dve.wait_ge(proj_evac, evacs[0])
                        if tile >= 2:
                            dve.wait_ge(silu_done, tile - 1)
                        w4 = v["conv_w"][:, 4 * tile:4 * tile + 4]
                        src, dst = conv_in[:, tile % 2, :], conv_acc[:, tile % 2, :]
                        step(V.tensor_scalar(dst, src[:, 0:T], w4[:, 0:1],
                                             v["conv_b"][:, tile:tile + 1], ALU.mult, ALU.add))
                        for j in range(1, 4):
                            ins = V.scalar_tensor_tensor(dst, src[:, j:j + T], w4[:, j:j + 1], dst,
                                                         ALU.mult, ALU.add)
                            if j < 3:
                                step(ins)
                            else:
                                ins.then_inc(conv_done, 1)
                    dve.wait_ge(conv_done, 2 * c + 2)
                elif c == N_XBC + N_Z:
                    dve.wait_ge(chunk_used, c + 1)
                    evac(k_t[:, P:], bank[b][:, :])
                elif c > N_XBC + N_Z:
                    dve.wait_ge(chunk_used, c + 1)
                    dve.wait_ge(dt_t_ps, 1)
                    for i in range(2):
                        evac(q_t[:, 2 * (c - N_XBC - N_Z - 1) + i, :], bank[b + i][:, :])

            for n in range(N_X):
                for j in range(4):
                    k = 4 * n + j
                    dve.wait_ge(xg_hi_done, k + 1)
                    V.scalar_tensor_tensor(xg_lo[:, k, :], ring[n][:, j * T:(j + 1) * T],
                                           v["norm_mix_g"][:, k:k + 1], f(xg_hi[:, k, :]),
                                           ALU.mult, ALU.subtract).then_inc(xg_lo_done, 1)
                if n == 0:
                    low(0)
            low(1)
            dve.wait_ge(sq_done, N_X)
            for half in (4, 2, 1):
                ins = V.tensor_tensor(sq[:, 0:half, :], sq[:, 0:half, :], sq[:, half:2 * half, :],
                                      ALU.add)
                if half > 1:
                    step(ins)
                else:
                    ins.then_inc(sq_summed, 1)
            dve.wait_ge(band_ps, 1)
            V.tensor_copy(band_rows[:, 0:FW], bank[7][0:HEADS, 0:FW]).then_inc(band_made, 1)
            dve.wait_ge(wdt_hi_done, 1)
            V.tensor_tensor(wdt_lo[:, :, :], wdt[:, :, :], f(wdt_hi[:, :, :]), ALU.subtract
                            ).then_inc(wdt_lo_done, 1)
            low(2)
            dve.wait_ge(ss_ps, 1)
            V.tensor_scalar(rstd_row[:, :], bank[6][:, :], 1.0 / D, EPS, ALU.mult, ALU.add
                            ).then_inc(ms_made, 1)
            dve.wait_ge(rms_root, 1)
            V.reciprocal(rstd_row[:, :], rstd_row[:, :]).then_inc(rstd_made, 1)
            dve.wait_ge(rstd_made, 1)
            dve.wait_ge(pads_made, 3)
            after_proj(0)
            for c in range(3, N_IN):
                low(c)
                if c == 3:
                    dve.wait_ge(rstd_t_ps, 1)
                    V.tensor_copy(rstd_tok[:, :], bank[7][:, :].rearrange("p (t q) -> p t q", t=TT)
                                  [:, :, 0]).then_inc(rstd_tok_made, 1)
                after_proj(c - 2)
                if c == 4:
                    dve.wait_ge(dt_ps, 1)
                    V.tensor_tensor(dt_row[:, :], bank[7][0:HEADS, :], rstd_row[0:HEADS, :], ALU.mult
                                    ).then_inc(dt_row_made, 1)
            dve.wait_ge(dt_t_ps, 1)
            row8 = lambda a: a.rearrange("p (o h) -> p o h", o=1).to_broadcast([P, TT, HEADS])
            th = lambda a: a[:, :].rearrange("p (t h) -> p t h", t=TT)
            step(V.tensor_tensor(th(dt_raw), bank[7][:, 0:32].rearrange("p (t h) -> p t h", t=TT),
                                 row8(v["dt_bias"]), ALU.add))
            V.scalar_tensor_tensor(dt_e[:, :], dt_raw[:, :], -1.0, dt_raw[:, :], ALU.mult, ALU.max
                                   ).then_inc(dt_arg, 1)
            dve.wait_ge(dt_exp, 1)
            V.tensor_scalar(dt_u[:, :], dt_e[:, :], 1.0, None, ALU.add).then_inc(dt_one, 1)
            dve.wait_ge(dt_one, 1)
            step(V.tensor_scalar(dt_d[:, :], dt_u[:, :], -1.0, None, ALU.add))
            step(V.tensor_tensor(dt_d[:, :], dt_e[:, :], dt_d[:, :], ALU.subtract))
            step(V.reciprocal(dt[:, :], dt_u[:, :]))
            step(V.tensor_tensor(dt_d[:, :], dt_d[:, :], dt[:, :], ALU.mult))
            dve.wait_ge(dt_log, 1)
            step(V.tensor_tensor(dt_l[:, :], dt_l[:, :], dt_d[:, :], ALU.add))
            step(V.tensor_scalar(dt_d[:, :], dt_raw[:, :], 0.0, None, ALU.max))
            step(V.tensor_tensor(dt[:, :], dt_d[:, :], dt_l[:, :], ALU.add))
            dve.wait_ge(a_exp, 1)
            step(V.tensor_scalar(a_neg[:, :], a_neg[:, :], -1.0, None, ALU.mult))
            V.tensor_tensor(th(adt), th(dt), row8(a_neg[:, :]), ALU.mult).then_inc(adt_made, 1)
            after_proj(N_IN - 2)
            dve.wait_ge(cum_ps, 1)
            V.tensor_copy(acum[:, :], bank[6][:, 0:32]).then_inc(cum_made, 1)
            V.tensor_copy(dtot[:, :], bank[6][:, 32:64]).then_inc(cum_made, 1)
            dve.wait_ge(cum_made, 2)
            V.tensor_tensor(dend[:, :], dtot[:, :], acum[:, :], ALU.subtract).then_inc(cum_made, 1)
            V.tensor_scalar(nacum[:, :], acum[:, :], -1.0, None, ALU.mult).then_inc(cum_made, 1)

            after_proj(N_IN - 1)
            dve.wait_ge(proj_evac, evacs[0])

            def softmax_in(a):
                n, j = a // 4, a % 4
                lo = P if n == 0 else 0
                s3 = psum[:, 4:6, 0:2 * P]
                if a >= 2:
                    dve.wait_ge(exp_made, 3 * (a - 1))
                dve.wait_ge(sc_ps, a + 1)
                V.scalar_tensor_tensor(scores[a % 2][:, :, lo:], s3[:, :, lo:], HD ** -0.5,
                                       bias[:, j::4, lo:], ALU.mult, ALU.add).then_inc(sc_read, 1)
                dve.wait_ge(sc_read, a + 1)
                sl = slice(2 * a, 2 * a + 2)
                step(V.tensor_reduce(smax[:, sl], scores[a % 2][:, :, lo:], AX.X, ALU.max))
                step(V.tensor_tensor(smax[:, sl], smax[:, sl], v["sinks"][:, j::4], ALU.max))
                step(V.tensor_tensor(sinkd[:, sl], v["sinks"][:, j::4], smax[:, sl], ALU.subtract))
                V.tensor_scalar(nmax[:, sl], smax[:, sl], -1.0, None, ALU.mult).then_inc(nmax_made, 1)

            def softmax_out(a):
                n, j = a // 4, a % 4
                sl = slice(2 * a, 2 * a + 2)
                dve.wait_ge(exp_made, 3 * a + 3)
                step(V.tensor_tensor(rden[:, sl], psums[:, sl], esink[:, sl], ALU.add))
                step(V.reciprocal(rden[:, sl], rden[:, sl]))
                dve.wait_ge(o_ps, a + 1)
                dst = mix[:, n, D_SSD:D].rearrange("p (i j d) -> p i j d", i=2, j=4)[:, :, j, :]
                V.tensor_tensor(dst, bank[7][:, 0:P].rearrange("p (i d) -> p i d", i=2),
                                rden[:, sl].rearrange("p (i o) -> p i o", o=1)
                                .to_broadcast([P, 2, HD]), ALU.mult).then_inc(o_read, 1)

            h3 = lambda a: a.rearrange("p (h d) -> p h d", h=HEADS)
            per_head = lambda a: a.rearrange("p (h o) -> p h o", o=1).to_broadcast([P, HEADS, HD])

            def scan(c, q):
                if q in (1, 2):
                    g = q - 1
                    dve.wait_ge(decay_made, 8 * c + 4 * g + 4)
                    dve.wait_ge(tok_made, 2 * c + 2)
                    if c:
                        dve.wait_ge(y_ps, c)
                    cb = bank[1][:, 256 + P * g:256 + P * g + P].rearrange("p (o l) -> p o l", o=1)
                    V.tensor_tensor(m_t[g][:, :, :], decay[g][:, :, :], cb.to_broadcast([P, 4, P]),
                                    ALU.mult).then_inc(m_made, 1)
                elif q == 3:
                    dve.wait_ge(y_ps, c + 1)
                    if c == 0:
                        V.tensor_copy(state[:, :], bank[0][:, :]).then_inc(state_made, 1)
                    elif c < TT - 1:
                        step(V.tensor_tensor(h3(state[:, :]), h3(state[:, :]),
                                             per_head(dtot[:, 8 * c:8 * c + 8]), ALU.mult))
                        V.tensor_tensor(state[:, :], state[:, :], bank[0][:, :], ALU.add
                                        ).then_inc(state_made, 1)
                    dve.wait_ge(xs_made, 3 * c + 3)
                    if c == 0:
                        step(V.tensor_tensor(y_tmp[:, :], bank[3][:, :], xskip[:, :], ALU.add))
                    else:
                        step(V.tensor_tensor(h3(y_tmp[:, :]), h3(bank[2][:, :]),
                                             per_head(eacum[:, 8 * c:8 * c + 8]), ALU.mult))
                        step(V.tensor_tensor(y_tmp[:, :], y_tmp[:, :], bank[3][:, :], ALU.add))
                        step(V.tensor_tensor(y_tmp[:, :], y_tmp[:, :], xskip[:, :], ALU.add))
                    V.tensor_tensor(mix[:, c, 0:D_SSD], y_tmp[:, :], zs[:, c, :], ALU.mult
                                    ).then_inc(y_read, 1)

            def norm(c):
                dve.wait_ge(ssq_made, 2 * c + 2)
                V.tensor_scalar(rms[:, 2 * c:2 * c + 2], ssq[:, 2 * c:2 * c + 2], 1.0 / 512, EPS,
                                ALU.mult, ALU.add).then_inc(mean_made, 1)

            dve.wait_ge(bias_loaded, 16)
            dve.wait_ge(cum_exp, 3)
            softmax_in(0)
            softmax_in(1)
            for a in range(16):
                c, q = a // 4, a % 4
                if a + 2 < 16:
                    softmax_in(a + 2)
                scan(c, q)
                softmax_out(a)
                if q == 1 and c:
                    norm(c - 1)
            norm(TT - 1)

            dve.wait_ge(pt_ps, 16)
            low(N_IN)
            for k in range(DK):
                dve.wait_ge(mix_hi_done, k + 1)
                V.scalar_tensor_tensor(mix_lo[:, k, :], bank[k][:, :], v["mix_g"][:, k:k + 1],
                                       f(mix_hi[:, k, :]), ALU.mult, ALU.subtract
                                       ).then_inc(mix_lo_done, 1)
            dve.wait_ge(h_loaded, 16)
            dve.wait_ge(trash_stored, 16)
            for i in range(N_OUT):
                if i + 1 < N_OUT:
                    low(N_IN + i + 1)
                else:
                    dve.wait_ge(router_loaded, 80)
                    V.tensor_tensor(wr[:, :, :], wr[:, :, :], v["norm_ffn_g"].rearrange(
                        "p (k o) -> p k o", o=1).to_broadcast([P, DK, E]), ALU.mult
                        ).then_inc(wr_scaled, 1)
                    for m in range(EARLY - 1):
                        low_of(dve, EXPERT_SLOT[m], LEAD + m + 1, (LEAD + m) % SPLITS)
                dve.wait_ge(chunk_used, N_IN + i + 1)
                for half in range(2):
                    dst = h[:, 2 * half:2 * half + 2, 256 * i:256 * i + 256]
                    V.tensor_tensor(dst, dst, bank[2 * i + half][:, :].rearrange("p (t c) -> p t c", t=2),
                                    ALU.add).then_inc(h_made, 1)
            router_dve(dve, mark, step, steps)
            moe_dve(dve)

        @block.tensor
        def _(pe):
            MM = nc.tensor.matmul

            def three(dst, xh, xl, wh, wl, first, last):
                MM(dst, xh, wh, start=first, stop=False)
                MM(dst, xl, wh, start=False, stop=False)
                return MM(dst, xh, wl, start=False, stop=last)

            for c in range(N_IN):
                wh, wl = w_hi[c % SPLITS], w_lo[c % SPLITS]
                w3h = wh[:, :].rearrange("p (k c) -> p k c", k=DK)
                w3l = wl[:, :].rearrange("p (k c) -> p k c", k=DK)
                if c == 3:
                    pe.wait_ge(proj_evac, 2)
                elif c in (4, 5, 6):
                    pe.wait_ge(proj_evac, 2 * (c - 2))
                elif c >= 7:
                    pe.wait_ge(z_made, 4 * (c - 6))
                pe.wait_ge(lo_done, c + 1)
                b = 2 * (c % 3)

                def channels(dst, cols):
                    for k in range(DK):
                        if c == 0 and cols.start == 0:
                            pe.wait_ge(xg_lo_done, k + 1)
                        i = MM(dst, w3h[:, k, cols], xg_hi[:, k, :], start=(k == 0), stop=False)
                        i = MM(dst, w3l[:, k, cols], xg_hi[:, k, :], start=False, stop=False)
                        i = MM(dst, w3h[:, k, cols], xg_lo[:, k, :], start=False, stop=(k == DK - 1))
                    return i

                def tokens(dst, t, wh3, wl3):
                    ts = slice(P * t, P * t + P)
                    for k in range(DK):
                        i = three(dst, xg_hi[:, k, ts], xg_lo[:, k, ts], wh3[:, k, :], wl3[:, k, :],
                                  k == 0, k == DK - 1)
                    return i

                if N_XBC <= c < N_XBC + N_Z:
                    for t in range(TT):
                        ins = tokens(bank[b + t // 2][:, 256 * (t % 2):256 * (t % 2) + 256], t, w3h, w3l)
                elif c == N_XBC + N_Z:
                    channels(bank[b][:, :], slice(0, P))
                    for t in range(TT):
                        ins = tokens(bank[b + 1][:, P * t:P * t + P], t, w3h[:, :, P:2 * P],
                                     w3l[:, :, P:2 * P])
                else:
                    channels(bank[b][:, :], slice(0, P))
                    ins = channels(bank[b + 1][:, :], slice(P, 2 * P))
                ins.then_inc(chunk_used, 1)
                if c == 0:
                    pe.wait_ge(const_loaded, 80)
                    MM(bank[7][0:HEADS, 0:FW], rel[:, :], band[:, 0:FW], start=True, stop=True
                       ).then_inc(band_ps, 1)
                    pe.wait_ge(sq_summed, 1)
                    MM(bank[6][:, :], const["ones"], sq[:, 0, :], start=True, stop=True
                       ).then_inc(ss_ps, 1)
                if c == 1:
                    pe.wait_ge(rstd_made, 1)
                    pe.wait_ge(band_made, 1)
                    for t in range(TT):
                        ins = nc.tensor.transpose(bank[7][:, P * t:P * t + P],
                                                  rstd_row[:, P * t:P * t + P], ident)
                    ins.then_inc(rstd_t_ps, 1)
                if c == 3:
                    pe.wait_ge(rstd_tok_made, 1)
                    pe.wait_ge(wdt_lo_done, 1)
                    for k in range(DK):
                        MM(bank[7][0:HEADS, :], wdt_hi[:, k, :], xg_hi[:, k, :], start=(k == 0),
                           stop=False)
                        MM(bank[7][0:HEADS, :], wdt_lo[:, k, :], xg_hi[:, k, :], start=False, stop=False)
                        ins = MM(bank[7][0:HEADS, :], wdt_hi[:, k, :], xg_lo[:, k, :], start=False,
                                 stop=(k == DK - 1))
                    ins.then_inc(dt_ps, 1)
                if c == N_IN - 2:
                    pe.wait_ge(incl_loaded, 16)
                    pe.wait_ge(adt_made, 1)
                    MM(bank[6][:, 0:32], incl[:, :], adt[:, :], start=True, stop=True)
                    MM(bank[6][:, 32:64], const["ones"], adt[:, :], start=True, stop=True
                       ).then_inc(cum_ps, 1)
                if c == 5:
                    pe.wait_ge(dt_row_made, 1)
                    for t in range(TT):
                        ins = nc.tensor.transpose(bank[7][:, HEADS * t:HEADS * t + HEADS],
                                                  dt_row[:, P * t:P * t + P], ident[0:HEADS, 0:HEADS])
                    ins.then_inc(dt_t_ps, 1)

            def attn_scores(a):
                n, j = a // 4, a % 4
                lo = P if n == 0 else 0
                if a:
                    pe.wait_ge(sc_read, a)
                for i in range(2):
                    ps = slice(HD * i, HD * i + HD)
                    ins = MM(bank[4 + i][:, lo:256], q_t[ps, j, P * n:P * n + P],
                             k_t[ps, P * n + lo:P * n + 256], start=True, stop=True)
                ins.then_inc(sc_ps, 1)

            def attn_turn(a):
                n = a // 4
                blocks = (1,) if n == 0 else (0, 1)
                pe.wait_ge(exp_made, 3 * a + 2)
                if a:
                    pe.wait_ge(pt_made, a)
                for i in range(2):
                    for kb in blocks:
                        w = 2 * i + kb if n else 2 + i
                        ins = nc.tensor.transpose(bank[6][:, P * w:P * w + P],
                                                  probs[a % 2][:, i, P * kb:P * kb + P], ident)
                ins.then_inc(pt_ps, 1)

            def attn_values(a):
                n = a // 4
                blocks = (1,) if n == 0 else (0, 1)
                pe.wait_ge(pt_made, a + 1)
                if a:
                    pe.wait_ge(o_read, a)
                for i in range(2):
                    for kb in blocks:
                        w = 2 * i + kb if n else 2 + i
                        ins = MM(bank[7][:, HD * i:HD * i + HD], probs_t[a % 2][:, w, :],
                                 v_tok[:, n + kb, HD * i:HD * i + HD], start=(kb == blocks[0]),
                                 stop=(kb == 1))
                ins.then_inc(o_ps, 1)

            def scan(c, q):
                cs = slice(P * c, P * c + P)
                if q == 0:
                    if c:
                        pe.wait_ge(state_made, c)
                        pe.wait_ge(m_made, 2 * c)
                    for i in range(4):
                        nc.tensor.transpose(bank[0][:, P * i:P * i + P], xbc[:, i, cs], ident)
                    for g in range(2):
                        nc.tensor.transpose(bank[1][:, P * g:P * g + P], xbc[:, 4 + g, cs], ident)
                    for g in range(2):
                        ins = MM(bank[1][:, 256 + P * g:256 + P * g + P], xbc[:, 4 + g, cs],
                                 xbc[:, 6 + g, cs], start=True, stop=True)
                    ins.then_inc(tok_ps, 1)
                if q in (1, 2):
                    g = q - 1
                    if 2 * c + g:
                        pe.wait_ge(decay_made, 4 * (2 * c + g))
                    if c:
                        pe.wait_ge(y_read, c)
                    MM(bank[2][:, :].rearrange("p (r l) -> p r l", r=4), ident_r[:, :],
                       negmask_r[:, :].rearrange("p (o l) -> p o l", o=1).to_broadcast([P, 4, P]),
                       start=True, stop=False)
                    for r in range(4):
                        jj = 8 * c + 4 * g + r
                        ins = MM(bank[2][:, P * r:P * r + P], adt[:, jj:jj + 1].to_broadcast([P, P]),
                                 incl[:, :], start=False, stop=(r == 3))
                    ins.then_inc(bc_ps, 1)
                if q in (2, 3):
                    g = q - 2
                    pe.wait_ge(m_made, 2 * c + g + 1)
                    pe.wait_ge(xs_made, 3 * c + 3)
                    if c:
                        pe.wait_ge(y_read, c)
                    for r in range(4):
                        hs = slice(HD * (4 * g + r), HD * (4 * g + r) + HD)
                        ins = MM(bank[3][:, hs], m_t[g][:, r, :], xdt[:, hs], start=True, stop=True)
                if q == 3:
                    if c:
                        pe.wait_ge(decay_made, 8 * c + 8)
                        for g in range(2):
                            ins = MM(bank[2][:, 256 * g:256 * g + 256], xbc[:, 6 + g, cs],
                                     state[:, 256 * g:256 * g + 256], start=True, stop=True)
                    if c < TT - 1:
                        for g in range(2):
                            ins = MM(bank[0][:, 256 * g:256 * g + 256], b_toks[c % 2][:, g, :],
                                     xdd[:, 256 * g:256 * g + 256], start=True, stop=True)
                    ins.then_inc(y_ps, 1)

            pe.wait_ge(proj_evac, 9)
            pe.wait_ge(v_made, 4)
            pe.wait_ge(silu_done, 8)
            scan(0, 0)
            pe.wait_ge(proj_evac, 13)
            attn_scores(0)
            attn_scores(1)
            pe.wait_ge(mask_rounded, 2)
            for a in range(16):
                attn_turn(a)
                if a + 2 < 16:
                    attn_scores(a + 2)
                if a:
                    scan(a // 4, a % 4)
                attn_values(a)

            pe.wait_ge(normed, 2 * TT - 2)
            for k in (0, 1, 4, 5, 6, 2, 3, 7):
                if k == 0:
                    pe.wait_ge(tok_made, 2 * TT)
                    pe.wait_ge(m_made, 2 * TT)
                elif k == 4:
                    pe.wait_ge(sc_read, 16)
                elif k == 6:
                    pe.wait_ge(pt_made, 16)
                elif k == 2:
                    pe.wait_ge(y_read, TT)
                elif k == 7:
                    pe.wait_ge(o_read, 16)
                for t in range(TT - 1):
                    nc.tensor.transpose(bank[k][:, P * t:P * t + P], mix[:, t, P * k:P * k + P], ident)
            pe.wait_ge(normed, 2 * TT)
            for k in range(DK):
                nc.tensor.transpose(bank[k][:, T - P:T], mix[:, TT - 1, P * k:P * k + P], ident
                                    ).then_inc(mix_ps, 1)
            for i in range(N_OUT):
                c = N_IN + i
                pe.wait_ge(lo_done, c + 1)
                w3h = w_hi[c % SPLITS][:, :].rearrange("p (k c) -> p k c", k=DK)
                w3l = w_lo[c % SPLITS][:, :].rearrange("p (k c) -> p k c", k=DK)
                for t in range(TT):
                    ts = slice(P * t, P * t + P)
                    for k in range(DK):
                        if i == 0 and t == 0:
                            pe.wait_ge(mix_lo_done, max(k + 1, 2))
                        ins = three(bank[2 * i + t // 2][:, 256 * (t % 2):256 * (t % 2) + 256],
                                    mix_hi[:, k, ts], mix_lo[:, k, ts], w3h[:, k, :], w3l[:, k, :],
                                    k == 0, k == DK - 1)
                ins.then_inc(chunk_used, 1)
            router_pe(pe, three)
            moe_pe(pe)


def kernel(x, norm_mix_g, w_in, conv_w, conv_b, dt_bias, a_log, d_skip, ssd_norm_g, attn_sinks,
           rel_bias, attn_norm_g, w_out, norm_ffn_g, w_router, b_router, w1, b1, w2, b2,
           norm_final_g):
    import concourse.bacc as bacc
    from concourse.bass_utils import run_bass_kernel_spmd

    x, w_in, w_out, w1, w2 = (np.asarray(a) for a in (x, w_in, w_out, w1, w2))
    f = np.float32
    o1, o2 = D_SSD, D_SSD + 2 * D_SSD
    o3 = o2 + HEADS
    o4 = o3 + D_SSD
    wi = w_in[0]
    q = wi[:, o3:o4].reshape(D, 2, 4, HD).transpose(0, 2, 1, 3).reshape(D, D_SSD)
    cols = np.concatenate([wi[:, o1:o2], wi[:, :o1], wi[:, o4:], q], 1)
    stream = np.empty((N_PRO + E * PER_EXPERT, P, CHUNK), f)
    stream[0:2] = x[0].T.reshape(2, 4, P, T).transpose(0, 2, 1, 3).reshape(2, P, CHUNK)
    stream[2:2 + N_IN] = cols.reshape(DK, P, N_IN, 256).transpose(2, 1, 0, 3).reshape(N_IN, P, CHUNK)
    stream[C_OUT:N_PRO] = w_out[0].reshape(DK, P, N_OUT, 256).transpose(2, 1, 0, 3).reshape(
        N_OUT, P, CHUNK)
    w1v = w1[0].reshape(E, 4, 2, P, 2, 2, 512).transpose(0, 5, 1, 3, 2, 4, 6)
    w2v = w2[0].reshape(E, 4, 2, P, D).transpose(0, 1, 3, 2, 4)
    moe = stream[N_PRO:]
    moe[0:4] = w1v[0, 0].reshape(4, P, CHUNK)
    for e in range(E):
        last = e == E - 1
        a = moe[4 + PER_EXPERT * e:]
        a[0:4] = w1v[e, 1].reshape(4, P, CHUNK)
        a[4:6] = w2v[e, 0:2].reshape(2, P, CHUNK)
        if not last:
            a[6:10] = w1v[e + 1, 0].reshape(4, P, CHUNK)
        k = 6 if last else 10
        a[k:k + 2] = w2v[e, 2:4].reshape(2, P, CHUNK)
    w_dt = np.ascontiguousarray(wi[:, o2:o3].reshape(DK, P, HEADS).transpose(1, 0, 2))

    def by_partition(a, n):
        return np.asarray(a).reshape(n, P).T

    def rows(a):
        return np.broadcast_to(np.asarray(a).reshape(1, -1), (P, np.asarray(a).size))

    parts = {
        "norm_mix_g": by_partition(norm_mix_g, DK),
        "conv_w": np.asarray(conv_w)[0].reshape(4, 8, P).transpose(2, 1, 0).reshape(P, 32),
        "conv_b": by_partition(conv_b, 8),
        "mix_g": np.concatenate([by_partition(ssd_norm_g, 4), by_partition(attn_norm_g, 4)], 1),
        "dt_bias": rows(dt_bias), "a_log": rows(a_log), "d_skip": rows(d_skip),
        "sinks": rows(attn_sinks), "b_router": rows(b_router),
        "norm_ffn_g": by_partition(norm_ffn_g, DK),
    }
    vectors = np.ascontiguousarray(np.concatenate([parts[n] for n, _ in VECTORS], 1))
    packed, where = shape_constants()
    order = MAIN_CONSTS + MIXER_CONSTS + ("band", "neg")
    consts = np.ascontiguousarray(np.concatenate(
        [packed[:, where[n][0]:where[n][0] + where[n][1]] for n in order], 1))
    arrays = {
        "stream": stream, "x": np.asarray(x)[0], "w_dt": w_dt, "vectors": vectors, "consts": consts,
        "rel_bias": rel_bias, "norm_ffn_g": np.asarray(norm_ffn_g)[0], "norm_final_g": norm_final_g,
        "w_router": np.asarray(w_router)[0], "b1": np.asarray(b1)[0], "b2": np.asarray(b2)[0],
    }
    arrays = {k: np.ascontiguousarray(a) for k, a in arrays.items()}
    nc = bacc.Bacc("TRN2", target_bir_lowering=False, num_devices=1)
    args = [nc.dram_tensor(k, a.shape, mybir.dt.from_np(a.dtype), kind="ExternalInput").ap()
            for k, a in arrays.items()]
    y = nc.dram_tensor("y", (T, D), F32, kind="ExternalOutput").ap()
    build(nc, *args, y)
    r = run_bass_kernel_spmd(nc, [arrays], core_ids=[0])
    return r.results[0]["y"].reshape(1, T, D)
```
